# Optimizing a Trainium2 kernel written in Bass

```python
import jax, jax.numpy as jnp
from jax import lax
import numpy as np

D_MODEL = 1024
BATCH = 1
SEQ = 1024
DEPTH = 1

MIX_WIDTH = 2 * D_MODEL
HEAD_DIM = 128
GDN_HEADS = 6
MLSTM_HEADS = 6
MEM_HEADS = 4
GDN_W = GDN_HEADS * HEAD_DIM
MLSTM_W = MLSTM_HEADS * HEAD_DIM
MEM_W = MEM_HEADS * HEAD_DIM
N_MEM = 256
CONV_WIDTH = 4
CHUNK = 64
EPS = 1e-6
SPLITS = [GDN_W, GDN_W, GDN_W, GDN_HEADS, GDN_HEADS, GDN_W,
          MLSTM_W, MLSTM_W, MLSTM_W, MLSTM_HEADS, MLSTM_HEADS, MLSTM_W, MLSTM_W,
          MEM_W, MEM_W]
IN_COLS = 4 * GDN_W + 2 * GDN_HEADS + 5 * MLSTM_W + 2 * MLSTM_HEADS + 2 * MEM_W

kernel_name = 'hybrid_gdn_mlstm_memxattn_block'

def rms_norm(x, g):
    xf = x.astype(jnp.float32)
    y = xf * lax.rsqrt(jnp.mean(xf * xf, axis=-1, keepdims=True) + EPS)
    return y * g.astype(jnp.float32)

def l2_normalize(x):
    return x * lax.rsqrt(jnp.sum(x * x, axis=-1, keepdims=True) + EPS)

def causal_depthwise_conv(x, w):
    k = w.shape[0]
    return lax.conv_general_dilated(x, w[:, None, :], window_strides=(1,), padding=[(k - 1, 0)],
                                    dimension_numbers=('NWC', 'WIO', 'NWC'),
                                    feature_group_count=x.shape[-1])

def to_chunks(x):
    b, t, h, d = x.shape
    return x.reshape(b, t // CHUNK, CHUNK, h, d).transpose(0, 3, 1, 2, 4)

def gate_to_chunks(x):
    b, t, h = x.shape
    return x.reshape(b, t // CHUNK, CHUNK, h).transpose(0, 3, 1, 2)

def from_chunks(x):
    b, h, nc, l, d = x.shape
    return x.transpose(0, 2, 3, 1, 4).reshape(b, nc * l, h, d)

def gated_delta_rule(q, k, v, g, beta):
    b_, h_, nc, l, d = q.shape
    causal = jnp.tril(jnp.ones((l, l), dtype=bool))
    strict = jnp.tril(jnp.ones((l, l), dtype=bool), -1)
    gc = jnp.cumsum(g, axis=-1)
    g_last = gc[..., -1]
    decay = jnp.exp(jnp.where(causal, gc[..., :, None] - gc[..., None, :], -jnp.inf))
    k_beta = k * beta[..., None]
    a_mat = jnp.where(strict, jnp.einsum('bhcid,bhcjd->bhcij', k_beta, k) * decay, 0.0)
    t_mat = a_mat + jnp.eye(l, dtype=q.dtype)
    u = lax.linalg.triangular_solve(t_mat, v * beta[..., None], left_side=True, lower=True,
                                    unit_diagonal=True)
    w = lax.linalg.triangular_solve(t_mat, k_beta * jnp.exp(gc)[..., None], left_side=True,
                                    lower=True, unit_diagonal=True)
    attn = jnp.einsum('bhcid,bhcjd->bhcij', q, k) * decay
    q_dec = q * jnp.exp(gc)[..., None]
    k_dec = k * jnp.exp(g_last[..., None] - gc)[..., None]
    xs = tuple(jnp.moveaxis(t, 2, 0) for t in (q_dec, w, u, attn, k_dec, jnp.exp(g_last)))

    def step(s, inp):
        q_c, w_c, u_c, a_c, k_c, gl_c = inp
        v_new = u_c - jnp.einsum('bhld,bhde->bhle', w_c, s)
        o = jnp.einsum('bhld,bhde->bhle', q_c, s) + jnp.einsum('bhlm,bhme->bhle', a_c, v_new)
        s = s * gl_c[..., None, None] + jnp.einsum('bhld,bhle->bhde', k_c, v_new)
        return s, o

    s0 = jnp.zeros((b_, h_, d, v.shape[-1]), q.dtype)
    _, o = lax.scan(step, s0, xs)
    return jnp.moveaxis(o, 0, 2)

def mlstm_chunkwise(q, k, v, log_i, log_f):
    b_, h_, nc, l, d = q.shape
    causal = jnp.tril(jnp.ones((l, l), dtype=bool))
    bcum = jnp.cumsum(log_f, axis=-1)
    b_last = bcum[..., -1]
    log_w = jnp.where(causal, bcum[..., :, None] - bcum[..., None, :] + log_i[..., None, :], -jnp.inf)
    m_intra = jnp.max(log_w, axis=-1)
    p = jnp.exp(log_w - m_intra[..., None]) * jnp.einsum('bhctd,bhcsd->bhcts', q, k)
    num_intra = jnp.einsum('bhcts,bhcsd->bhctd', p, v)
    den_intra = jnp.sum(p, axis=-1)
    log_end = b_last[..., None] - bcum + log_i
    m_loc = jnp.max(log_end, axis=-1)
    k_end = k * jnp.exp(log_end - m_loc[..., None])[..., None]
    xs = tuple(jnp.moveaxis(t, 2, 0) for t in
               (q, k_end, v, bcum, b_last, m_intra, num_intra, den_intra, m_loc))

    def step(carry, inp):
        c_st, n_st, m_st = carry
        q_c, k_c, v_c, b_c, bl_c, mi_c, ni_c, di_c, ml_c = inp
        m_t = jnp.maximum(b_c + m_st[..., None], mi_c)
        a = jnp.exp(b_c + m_st[..., None] - m_t)
        r = jnp.exp(mi_c - m_t)
        num = a[..., None] * jnp.einsum('bhld,bhde->bhle', q_c, c_st) + r[..., None] * ni_c
        den = a * jnp.einsum('bhld,bhd->bhl', q_c, n_st) + r * di_c
        h = num / jnp.maximum(jnp.abs(den), jnp.exp(-m_t))[..., None]
        m_new = jnp.maximum(bl_c + m_st, ml_c)
        s_old = jnp.exp(bl_c + m_st - m_new)
        s_loc = jnp.exp(ml_c - m_new)
        c_st = s_old[..., None, None] * c_st + s_loc[..., None, None] * jnp.einsum('bhld,bhle->bhde', k_c, v_c)
        n_st = s_old[..., None] * n_st + s_loc[..., None] * jnp.sum(k_c, axis=-2)
        return (c_st, n_st, m_new), h

    init = (jnp.zeros((b_, h_, d, d), q.dtype), jnp.zeros((b_, h_, d), q.dtype),
            jnp.zeros((b_, h_), q.dtype))
    _, h = lax.scan(step, init, xs)
    return jnp.moveaxis(h, 0, 2)

def setup_inputs(seed: int = 0) -> dict:
    key = jax.random.key(seed)
    ks = jax.random.split(key, 16)
    f32 = jnp.float32
    nrm = jax.random.normal
    x = nrm(ks[0], (BATCH, SEQ, D_MODEL), f32)
    mem = nrm(ks[1], (BATCH, N_MEM, D_MODEL), f32)
    norm_g = 1.0 + 0.02 * nrm(ks[2], (DEPTH, D_MODEL), f32)
    w_in = nrm(ks[3], (DEPTH, D_MODEL, IN_COLS), f32) * D_MODEL ** -0.5
    conv_w = nrm(ks[4], (DEPTH, CONV_WIDTH, 3 * GDN_W), f32) * CONV_WIDTH ** -0.5
    gdn_a_log = jnp.log(jax.random.uniform(ks[5], (DEPTH, GDN_HEADS), f32, minval=1.0, maxval=16.0))
    dt = jnp.exp(jax.random.uniform(ks[6], (DEPTH, GDN_HEADS), f32,
                                    minval=math_log(1e-3), maxval=math_log(1e-1)))
    gdn_dt_bias = dt + jnp.log(-jnp.expm1(-dt))
    gdn_norm_g = 1.0 + 0.02 * nrm(ks[7], (DEPTH, HEAD_DIM), f32)
    mlstm_i_bias = 0.1 * nrm(ks[8], (DEPTH, MLSTM_HEADS), f32)
    mlstm_f_bias = jax.random.uniform(ks[9], (DEPTH, MLSTM_HEADS), f32, minval=3.0, maxval=6.0)
    mlstm_norm_g = 1.0 + 0.02 * nrm(ks[10], (DEPTH, MLSTM_HEADS, HEAD_DIM), f32)
    mem_norm_g = 1.0 + 0.02 * nrm(ks[11], (DEPTH, D_MODEL), f32)
    w_mem_kv = nrm(ks[12], (DEPTH, D_MODEL, 2 * MEM_W), f32) * D_MODEL ** -0.5
    w_out = nrm(ks[13], (DEPTH, MIX_WIDTH, D_MODEL), f32) * MIX_WIDTH ** -0.5
    final_norm_g = 1.0 + 0.02 * nrm(ks[14], (D_MODEL,), f32)
    return {'x': x, 'mem': mem, 'norm_g': norm_g, 'w_in': w_in, 'conv_w': conv_w,
            'gdn_a_log': gdn_a_log, 'gdn_dt_bias': gdn_dt_bias, 'gdn_norm_g': gdn_norm_g,
            'mlstm_i_bias': mlstm_i_bias, 'mlstm_f_bias': mlstm_f_bias, 'mlstm_norm_g': mlstm_norm_g,
            'mem_norm_g': mem_norm_g, 'w_mem_kv': w_mem_kv, 'w_out': w_out,
            'final_norm_g': final_norm_g}

def math_log(v):
    return float(np.log(v))

def reference(x, mem, norm_g, w_in, conv_w, gdn_a_log, gdn_dt_bias, gdn_norm_g,
              mlstm_i_bias, mlstm_f_bias, mlstm_norm_g, mem_norm_g, w_mem_kv, w_out,
              final_norm_g):
    f32 = jnp.float32
    bsz, seq, _ = x.shape
    split_idx = [int(c) for c in np.cumsum(SPLITS)[:-1]]
    h_res = x.astype(f32)
    for layer in range(DEPTH):
        hn = rms_norm(h_res, norm_g[layer])
        proj = hn @ w_in[layer].astype(f32)
        (g_q, g_k, g_v, g_a, g_b, g_z,
         m_q, m_k, m_v, m_i, m_f, m_o, m_z,
         x_q, x_z) = jnp.split(proj, split_idx, axis=-1)

        qkv = jax.nn.silu(causal_depthwise_conv(jnp.concatenate([g_q, g_k, g_v], axis=-1),
                                                conv_w[layer].astype(f32)))
        cq, ck, cv = jnp.split(qkv, 3, axis=-1)
        cq = l2_normalize(cq.reshape(bsz, seq, GDN_HEADS, HEAD_DIM)) * HEAD_DIM ** -0.5
        ck = l2_normalize(ck.reshape(bsz, seq, GDN_HEADS, HEAD_DIM))
        cv = cv.reshape(bsz, seq, GDN_HEADS, HEAD_DIM)
        g_log = -jnp.exp(gdn_a_log[layer].astype(f32)) * jax.nn.softplus(g_a + gdn_dt_bias[layer].astype(f32))
        beta = jax.nn.sigmoid(g_b)
        o_gdn = gated_delta_rule(to_chunks(cq), to_chunks(ck), to_chunks(cv),
                                 gate_to_chunks(g_log), gate_to_chunks(beta))
        o_gdn = rms_norm(from_chunks(o_gdn), gdn_norm_g[layer]).reshape(bsz, seq, GDN_W)
        o_gdn = o_gdn * jax.nn.silu(g_z)

        mq = m_q.reshape(bsz, seq, MLSTM_HEADS, HEAD_DIM)
        mk = m_k.reshape(bsz, seq, MLSTM_HEADS, HEAD_DIM) * HEAD_DIM ** -0.5
        mv = m_v.reshape(bsz, seq, MLSTM_HEADS, HEAD_DIM)
        log_i = m_i + mlstm_i_bias[layer].astype(f32)
        log_f = jax.nn.log_sigmoid(m_f + mlstm_f_bias[layer].astype(f32))
        h_ml = mlstm_chunkwise(to_chunks(mq), to_chunks(mk), to_chunks(mv),
                               gate_to_chunks(log_i), gate_to_chunks(log_f))
        h_ml = from_chunks(h_ml) * jax.nn.sigmoid(m_o).reshape(bsz, seq, MLSTM_HEADS, HEAD_DIM)
        h_ml = rms_norm(h_ml, mlstm_norm_g[layer]).reshape(bsz, seq, MLSTM_W)
        h_ml = h_ml * jax.nn.silu(m_z)

        mem_n = rms_norm(mem, mem_norm_g[layer])
        kv = mem_n @ w_mem_kv[layer].astype(f32)
        mem_k, mem_v = jnp.split(kv, 2, axis=-1)
        mem_k = mem_k.reshape(bsz, -1, MEM_HEADS, HEAD_DIM)
        mem_v = mem_v.reshape(bsz, -1, MEM_HEADS, HEAD_DIM)
        xq = x_q.reshape(bsz, seq, MEM_HEADS, HEAD_DIM)
        scores = jnp.einsum('bthd,bmhd->bhtm', xq, mem_k) * HEAD_DIM ** -0.5
        probs = jax.nn.softmax(scores, axis=-1)
        o_mem = jnp.einsum('bhtm,bmhd->bthd', probs, mem_v).reshape(bsz, seq, MEM_W)
        o_mem = o_mem * jax.nn.silu(x_z)

        mixed = jnp.concatenate([o_gdn, h_ml, o_mem], axis=-1)
        h_res = h_res + mixed @ w_out[layer].astype(f32)
    return rms_norm(h_res, final_norm_g).astype(x.dtype)


_drawn_inputs = setup_inputs


def setup_inputs(seed=0):
    import zlib

    import numpy as np

    out = dict(_drawn_inputs(seed))
    spreads = {}
    factors = {'norm_g': 2.989,
     'gdn_a_log': 3.04,
     'gdn_norm_g': 136.571,
     'mlstm_i_bias': 64.0,
     'mlstm_norm_g': 149.86,
     'mem_norm_g': 36.602,
     'final_norm_g': 23.864}
    for name, (base, spread) in spreads.items():
        noise = np.random.default_rng([zlib.crc32(name.encode()), seed]).standard_normal(out[name].shape)
        drawn = base * np.exp(spread * noise) if base else spread * noise
        out[name] = __import__('jax').numpy.asarray(drawn.astype(out[name].dtype))
    for name, factor in factors.items():
        out[name] = (out[name] * factor).astype(out[name].dtype)
    return out
```

```python
from contextlib import ExitStack

import concourse.bass as bass
import numpy as np
from concourse import mybir

F32 = mybir.dt.float32
F32R = mybir.dt.float32r
ALU = mybir.AluOpType
ACT = mybir.ActivationFunctionType
AX = mybir.AxisListType

P = 128
D_MODEL = 1024
SEQ = 1024
N_MEM = 256
MIX = 2 * D_MODEL
KT = D_MODEL // P
NC = SEQ // P
HALF = 512
GH, MH, XH = 6, 6, 4
HEADS = GH + MH + XH
GW, MW, XW = GH * P, MH * P, XH * P
EPS = 1e-6
SCALE = float(P) ** -0.5
WIDTHS = [GW, GW, GW, GH, GH, GW, MW, MW, MW, MH, MH, MW, MW, XW, XW]
(G_Q, G_K, G_V, G_A, G_B, G_Z, M_Q, M_K, M_V, M_I, M_F, M_O, M_Z, X_Q, X_Z, IN_COLS) = \
    [int(v) for v in np.cumsum([0] + WIDTHS)]
GDN, MLSTM, MEM = range(3)
BLOCKS = {GDN: [G_Q, G_K, G_V, G_Z], MLSTM: [M_Q, M_K, M_V, M_O, M_Z], MEM: [X_Q, X_Z]}
SLOTS = {GDN: [0, 1, 0, 1], MLSTM: [0, 1, 2, 0, 1], MEM: [0, 1]}
TERMS = 3
UNIT = KT * TERMS
LEVELS = 7
R_GA, R_MF, R_GB, R_MI = 0, 32, 64, 96
T_G, T_E, T_F, T_L, T_X, T_NE, NTAB = 0, 1, 2, 3, 4, 5, 6
PAST = 3


def uses(slot, head, block):
    kind, h = head
    n = SLOTS[kind][:block + 1].count(slot)
    if slot == 2:
        return 1 + h + n
    return {GDN: 2 * h, MLSTM: 2 * GH + 2 * h, MEM: 2 * GH + 2 * MH + h}[kind] + n + KV_USES


KV_USES = 4
UNITS = {GDN: 8, MLSTM: 10, MEM: 4}


def units_before(head):
    kind, h = head
    return PRE_UNITS + {GDN: 8 * h, MLSTM: 8 * GH + 10 * h, MEM: 8 * GH + 10 * MH + 4 * h}[kind]


PRE_UNITS = 2 * XH + 2

FILL = {
    GDN: [("decay", 32), ("sums", 48), ("pairs", 8)] + [(f"a{l}", 3) for l in range(LEVELS)]
         + [(f"b{l}", 3) for l in range(1, LEVELS)]
         + [(f"{s}{c}", n) for c in range(NC) for s, n in (("r", 3), ("y", 2), ("s", 2))] + [("turn", 9)],
    MLSTM: [("v", 16), ("decay", 16), ("pairs", 24), ("k", 16), ("o", 16)]
           + [(f"c{c}", 8) for c in range(NC)] + [("turn", 24)],
    MEM: [("v", 8), ("scores", 8), ("probs", 40), ("out", 24)],
}


def order(kind):
    if kind == GDN:
        s = ["decay", "sums", "pairs", "a0"]
        for l in range(1, LEVELS):
            s += [f"a{l}", f"b{l}"]
        for c in range(NC):
            s += [f"r{c}", f"y{c}", f"s{c}"]
        return s + ["turn"]
    if kind == MLSTM:
        return ["v", "decay", "pairs", "k", "o"] + [f"c{c}" for c in range(NC)] + ["turn"]
    return ["v", "scores", "probs", "out"]


def plan(kind, nxt):
    total = UNITS[nxt] * UNIT if nxt is not None else 0
    fill, done, out = dict(FILL[kind]), 0, {}
    for s in order(kind):
        done = min(total, done + fill[s])
        out[s] = done
    out["end"] = total
    return out



class Steps:

    def __init__(self, eng, sem, base=0):
        self.eng, self.sem, self.base, self.n = eng, sem, base, 0

    def done(self, ins):
        self.n += 1
        ins.then_inc(self.sem, 1)
        self.eng.wait_ge(self.sem, self.base + self.n)


def build(nc, x, mem, norm_g, w_in, conv_w, a_log, dt_bias, gdn_g, i_bias, f_bias, mlstm_g,
          mem_g, w_kv, w_out, final_g, out, mixed):
    ctx = ExitStack()
    with ctx:
        place = [16640]

        def sb(name, shape, dt=F32, offset=None):
            size = (4 * int(np.prod(shape[1:])) + 31) // 32 * 32
            if offset is None:
                offset = place[0]
                place[0] += size
            return nc.alloc_sbuf_tensor_at(name, shape, dt, offset=offset)

        def sem(name):
            return ctx.enter_context(nc.semaphore(name))

        def flat(t):
            return t[:, :, :, :].rearrange("p a b c -> p (a b c)")

        def over(ap, n):
            return ap.unsqueeze(2).broadcast_to([P, ap.shape[1], n])

        def each(ap, n):
            return ap.unsqueeze(1).broadcast_to([P, n, ap.shape[1]])

        ident = sb("ident", [P, P])
        upper = sb("upper", [P, P])
        later = sb("later", [P, P])
        ones = sb("ones", [P, P])
        first_t = sb("first_t", [P, P])
        level_mask = sb("level_mask", [P, LEVELS, 64])
        minus_half = sb("minus_half", [P, 16])
        param_rows = sb("param_rows", [80, P])
        params = sb("params", [P, 80])
        gcol = sb("gcol", [P, 4])
        tab = sb("tab", [P, GH + MH, NTAB, NC])
        guard = sb("guard", [P, MH, NC])
        ht = sb("ht", [P, NTAB, NC])
        hguard = sb("hguard", [P, NC])
        hconv = sb("hconv", [P, 12])
        hnorm = sb("hnorm", [P, 1])
        ss_tiles = sb("ss_tiles", [P, 16])
        rstd_tiles = sb("rstd_tiles", [P, 16])
        sm = sb("sm", [P, 12, 16])
        state = sb("state", [P, P + 1])
        rhs = sb("rhs", [P, 2, P])
        zed = sb("zed", [P, 2, P])
        carried = sb("carried", [P, 2, P + 1])
        kv_at = place[0]
        kv = sb("kv", [P, 2 * XH, N_MEM])
        hkv = sb("hkv", [P, 2, N_MEM])
        vm = sb("vm", [P, 2, P])
        xn_hi = sb("xn_hi", [P, KT, SEQ], F32R)
        xn_lo = sb("xn_lo", [P, KT, SEQ], F32R)
        late_at = place[0]
        w_raw = [sb(f"w_raw{s}", [P, KT, P]) for s in range(3)]
        w_hi = [sb(f"w_hi{s}", [P, KT, P], F32R) for s in range(3)]
        w_lo = [sb(f"w_lo{s}", [P, KT, P], F32R) for s in range(3)]
        raw = sb("raw", [P, 5, PAST + SEQ])
        work_at = place[0]
        qk = sb("qk", [P, NC, 2, P])
        vt = sb("vt", [P, SEQ])
        sz = sb("sz", [P, SEQ])
        gu = sb("gu", [P, NC, P])
        dd = sb("dd", [P, NC, 2, P])
        pair = sb("pair", [P, NC, 2, P])
        minv_at = place[0]
        minv = sb("minv", [P, NC, P])
        minv_t = sb("minv_t", [P, NC, P])
        xx_at = place[0]
        xx = [sb(f"xx{i}", [P, NC, P]) for i in range(2)]
        fk = sb("fk", [P, NC, P])
        nv = sb("nv", [P, NC, P])
        mix = sb("mix", [P, SEQ])
        work_end = place[0]
        assert work_end <= 229368, work_end
        v_ext = sb("v_ext", [P, NC, P + 1], offset=minv_at)
        num_den = sb("num_den", [P, NC, P + 1], offset=xx_at)
        spot = [work_at]

        def early(name, shape, dt=F32):
            t = sb(name, shape, dt, offset=spot[0])
            spot[0] += (4 * int(np.prod(shape[1:])) + 31) // 32 * 32
            assert spot[0] <= work_end, name
            return t

        mem_hi = early("mem_hi", [P, KT, N_MEM], F32R)
        mem_lo = early("mem_lo", [P, KT, N_MEM], F32R)
        g_rows = early("g_rows", [P, 2, D_MODEL])
        x_in = early("x_in", [P, 2, D_MODEL])
        x_tok = early("x_tok", [P, 2, D_MODEL])
        rows = early("rows", [P, SEQ])
        z_row = early("z_row", [P, SEQ])
        m_row = early("m_row", [P, SEQ + 8])
        i_row, u_row = x_in[:, 0, :], x_in[:, 1, :]
        e_row, l_row = x_tok[:, 0, :], x_tok[:, 1, :]
        junk = early("junk", [P, SEQ - 8])
        spot[0] = late_at
        wo_hi = [xn_hi, early("wo_hi", [P, KT, D_MODEL], F32R)]
        wo_lo = [xn_lo, early("wo_lo", [P, KT, D_MODEL], F32R)]
        mx_raw = early("mx_raw", [P, 16, P])
        mx_hi = [early(f"mx_hi{i}", [P, 16, P], F32R) for i in range(2)]
        mx_lo = [early(f"mx_lo{i}", [P, 16, P], F32R) for i in range(2)]
        wo_raw = [early(f"wo_raw{i}", [P, D_MODEL]) for i in range(2)]
        y = early("y", [P, D_MODEL])
        x_t = early("x_t", [P, D_MODEL])
        fg_row = sb("fg_row", [P, D_MODEL], offset=kv_at)
        y_sq = sb("y_sq", [P, D_MODEL], offset=kv_at + 4 * D_MODEL)

        ps = nc.alloc_psum_tensor("ps", [P, 8, HALF], F32)

        names = """consts tiny g_zero gw_zero x_loaded0 x_loaded1 x_square x_rstd x_scaled x_turned x_hi
            x_lo rowz_loaded grows gate_act gate_rows gate_turned gate_tab gate_sum gate_exp gate_m
            gate_beta pool_early pool_turn params_turned params_out unit_done unit_out head_done mix_stored
            g_tab g_conv g_silu g_sq g_gu g_ss g_sse g_rk g_w g_decay g_exp g_dd g_kq g_pair g_kt g_fk
            g_vt g_nv g_mt0 g_m0 g_a g_x g_b g_m g_c g_mt g_xz g_ks g_qs g_r g_y g_z g_up g_att g_s
            g_cq g_o g_osq g_oms g_ors g_og g_ot g_dve
            m_tab m_qk m_sig m_gate m_gu m_v m_ve m_decay m_exp m_dd m_pair m_pm m_k m_fk m_o m_sg
            m_up m_s m_qc m_cq m_pv m_nd m_h m_hsq m_ms m_rs m_og m_ot m_dve
            x_kv x_q x_silu x_v x_vm x_sc x_max x_nb x_p x_pn x_pt x_ptc x_o x_dve
            o_load0 o_load1 o_hi0 o_hi1 o_lo0 o_lo1 o_fg o_mx o_mhi o_mlo o_x o_y o_ps o_sq o_ms o_rs
            o_out o_st early_dve early_pool early_act""".split()
        S = {n: sem(n) for n in names}
        w_loaded = [sem(f"w_loaded{s}") for s in range(3)]
        w_hi_done = [sem(f"w_hi_done{s}") for s in range(3)]
        w_split = [sem(f"w_split{s}") for s in range(3)]

        w_cols = w_in.rearrange("(k p) n -> p k n", p=P)
        kv_cols = w_kv.rearrange("(k p) n -> p k n", p=P)
        TILES = [(mem, 0), (mem, 1)] + [(x, t) for t in range(NC)]

        def halves(t, l):
            v = t[:, :, :].rearrange("p c (n two b) -> p c n two b", two=2, b=1 << l)
            return v[:, :, :, 0, :], v[:, :, :, 1, :]

        def halves_of(t, c, l):
            v = t[:, c, :].rearrange("p (n two b) -> p n two b", two=2, b=1 << l)
            return v[:, :, 0, :], v[:, :, 1, :]

        def packed(bank, l):
            return ps[:, bank, :].rearrange("p (c n b) -> p c n b", c=NC, b=1 << l)

        block = ctx.enter_context(nc.Block())

        @block.sync
        def _(sp):
            def load(slot, n, src):
                if n is not None:
                    sp.wait_ge(w_split[slot], n)
                sp.dma_start(w_raw[slot][:, :, :], src).then_inc(w_loaded[slot], 16)

            def head_blocks(kind, h):
                for b, (first, slot) in enumerate(zip(BLOCKS[kind], SLOTS[kind])):
                    load(slot, uses(slot, (kind, h), b) - 1,
                         w_cols[:, :, bass.ds(h * P + first, P)])

            def x_tile(i):
                src, t = TILES[i]
                if i >= 2:
                    sp.wait_ge(S["x_scaled"], i - 1)
                sp.dma_start(x_in[:, i % 2, :], src[t * P:(t + 1) * P, :]).then_inc(S[f"x_loaded{i % 2}"], 16)

            x_tile(0)
            x_tile(1)
            for r, g in enumerate((norm_g, mem_g)):
                sp.dma_start(g_rows[:, r, :], g.partition_broadcast(P)).then_inc(S["grows"], 16)
            for b in range(2):
                load(b, None, kv_cols[:, :, b * P:(b + 1) * P])
            sp.wait_ge(S["gw_zero"], 1)
            for first, row in ((G_A, R_GA), (M_F, R_MF), (G_B, R_GB), (M_I, R_MI)):
                sp.dma_start(w_raw[2][:, :, row:row + GH], w_cols[:, :, first:first + GH])\
                    .then_inc(w_loaded[2], 16)
            for src, row, col in ((dt_bias, R_GA, 1), (f_bias, R_MF, 1), (a_log, R_GA, 2), (i_bias, R_MF, 3)):
                sp.dma_start(gcol[row:row + GH, col:col + 1], src.rearrange("(h a) -> h a", a=1))\
                    .then_inc(S["tiny"], 16)
            taps = conv_w.shape[0] * conv_w.shape[1] // P
            for r in range(conv_w.shape[0]):
                n = conv_w.shape[1] // P
                sp.dma_start(param_rows[r * n:(r + 1) * n, :], conv_w[r].rearrange("(b p) -> b p", p=P))\
                    .then_inc(S["rowz_loaded"], 16)
            sp.dma_start(param_rows[taps:taps + 1, :], gdn_g.rearrange("(a p) -> a p", a=1))\
                .then_inc(S["rowz_loaded"], 16)
            sp.dma_start(param_rows[taps + 1:taps + 1 + MH, :], mlstm_g).then_inc(S["rowz_loaded"], 16)
            for i in range(2, 2 + NC):
                x_tile(i)
                if 4 <= i:
                    b = i - 2
                    load(b % 2, b // 2, kv_cols[:, :, b * P:(b + 1) * P])
            head_blocks(GDN, 0)
            with sp.Fori(1, GH) as h:
                head_blocks(GDN, h)
            with sp.Fori(0, MH) as h:
                head_blocks(MLSTM, h)
            with sp.Fori(0, XH) as h:
                head_blocks(MEM, h)

            sp.wait_ge(S["head_done"], HEADS + 1)
            sp.dma_start(fg_row[:, :], final_g.partition_broadcast(P)).then_inc(S["o_fg"], 16)
            for i in range(KT):
                for j in range(2):
                    if i:
                        sp.wait_ge(S[f"o_lo{j}"], i)
                    kt = j * KT + i
                    sp.dma_start(wo_raw[j][:, :], w_out[kt * P:(kt + 1) * P, :]).then_inc(S[f"o_load{j}"], 16)
                if i == 0:
                    sp.wait_ge(S["mix_stored"], 16 * (HEADS + 1))
                    sp.dma_start(mx_raw[:, :, :], mixed[:, 0:P].rearrange("(k p) t -> p k t", p=P))\
                        .then_inc(S["o_mx"], 16)
                    sp.dma_start(x_t[:, :], x[0:P, :]).then_inc(S["o_x"], 16)
            for t in range(NC):
                if t + 1 < NC:
                    sp.wait_ge(S["o_mlo"], t + 1)
                    sp.dma_start(mx_raw[:, :, :], mixed[:, (t + 1) * P:(t + 2) * P].rearrange("(k p) t -> p k t", p=P))\
                        .then_inc(S["o_mx"], 16)
                    sp.wait_ge(S["o_y"], 2 * (t + 1))
                    sp.dma_start(x_t[:, :], x[(t + 1) * P:(t + 2) * P, :]).then_inc(S["o_x"], 16)
                sp.wait_ge(S["o_out"], t + 1)
                sp.dma_start(out[t * P:(t + 1) * P, :], y[:, :]).then_inc(S["o_st"], 16)
            sp.wait_ge(S["o_st"], 16 * NC)

        @block.gpsimd
        def _(pool):
            def split_hi(slot, n, loaded, free):
                pool.wait_ge(w_loaded[slot], loaded)
                if free is not None:
                    pool.wait_ge(S["unit_done"], free)
                plain()
                pool.tensor_copy(w_hi[slot][:, :, :], w_raw[slot][:, :, :]).then_inc(w_hi_done[slot], 1)

            def plain():
                pool.sem_inc(S["pool_turn"], 1)

            early = Steps(pool, S["early_pool"])
            pool.memset(gcol[:, :], 0.0)
            pool.memset(w_raw[2][:, :, :], 0.0).then_inc(S["gw_zero"], 1)
            pool.memset(minus_half[:, :], -0.5)
            early.done(pool.memset(ones[:, :], 1.0))
            pool.affine_select(out=upper[:, :], in_=ones[:, :], compare_op=ALU.is_ge, fill=0.0, base=0,
                               pattern=[[1, P]], channel_multiplier=-1)
            early.done(pool.affine_select(out=later[:, :], in_=ones[:, :], compare_op=ALU.is_gt, fill=0.0, base=0,
                                          pattern=[[-1, P]], channel_multiplier=1))
            early.done(pool.affine_select(out=ident[:, :], in_=upper[:, :], compare_op=ALU.is_ge, fill=0.0, base=0,
                                          pattern=[[-1, P]], channel_multiplier=1))
            pool.memset(level_mask[:, :, :], -1.0)
            early.done(pool.memset(first_t[:, :], -1.0))
            ft = first_t[:, :].rearrange("p (n r) -> p n r", r=2)
            early.done(pool.affine_select(out=ft, in_=ft, compare_op=ALU.is_equal, fill=0.0, base=0,
                                          pattern=[[-2, P // 2], [0, 2]], channel_multiplier=1))
            early.done(pool.affine_select(out=ft, in_=ft, compare_op=ALU.is_gt, fill=0.0, base=0,
                                          pattern=[[0, P // 2], [1, 2]], channel_multiplier=0))
            for l in range(LEVELS):
                b = 1 << l
                m = level_mask[:, l, :].rearrange("p (n r) -> p n r", r=b)
                early.done(pool.affine_select(out=m, in_=m, compare_op=ALU.is_ge, fill=0.0, base=-b,
                                              pattern=[[-2 * b, 64 // b], [0, b]], channel_multiplier=1))
                early.done(pool.affine_select(out=m, in_=m, compare_op=ALU.is_ge, fill=0.0, base=2 * b - 1,
                                              pattern=[[2 * b, 64 // b], [0, b]], channel_multiplier=-1))
            pool.memset(rows[:, :], 0.0)
            pool.memset(m_row[:, :], 0.0)
            pool.memset(raw[:, 0:3, 0:PAST], 0.0).then_inc(S["consts"], 1)

            for i in range(2 + NC):
                pool.wait_ge(S["x_square"], i + 1)
                early.done(pool.tensor_scalar(ss_tiles[:, i:i + 1], ss_tiles[:, i:i + 1], 1.0 / D_MODEL, EPS,
                                              ALU.mult, ALU.add))
                pool.tensor_tensor(rstd_tiles[:, i:i + 1], ss_tiles[:, i:i + 1], minus_half[:, 0:1], ALU.pow)\
                    .then_inc(S["x_rstd"], 1)
                if 1 <= i <= 2 * XH:
                    b = i - 1
                    split_hi(b % 2, b // 2 + 1, 16 * (b // 2 + 1), b - 1 if b >= 2 else None)
            split_hi(2, 1, 64, None)
            for slot in range(2):
                split_hi(slot, KV_USES + 1, 16 * (KV_USES + 1), 2 * XH - 1 + slot)

            def start_split(nxt):
                if nxt is not None and nxt[0] == MLSTM:
                    n = uses(2, nxt, 2)
                    split_hi(2, n, 48 + n * 16, units_before(nxt) - 4)

            def gdn(h, nxt):
                pool.wait_ge(S["g_tab"], h + 1)
                pool.tensor_tensor(gu[:, :, :], each(upper[:, :], NC), over(ht[:, T_G, :], P), ALU.mult)\
                    .then_inc(S["g_gu"], 1)
                start_split(nxt)
                plain()
                pool.memset(xx[0][:, :, :], 0.0).then_inc(S["g_xz"], 1)
                pool.tensor_copy(minv[:, :, :], each(ident[:, :], NC)).then_inc(S["g_m0"], 1)
                pool.wait_ge(S["g_sse"], h + 1)
                pool.tensor_tensor(sm[:, 1, :], sm[:, 0, :], minus_half[:, :], ALU.pow).then_inc(S["g_rk"], 1)
                pool.wait_ge(S["g_dd"], h + 1)
                plain()
                pool.memset(xx[1][:, :, :], 0.0).then_inc(S["g_xz"], 1)
                pool.wait_ge(S["g_pair"], 4 * h + 4)
                pool.tensor_tensor(minv_t[:, :, :], pair[:, :, 0, :], each(first_t[:, :], NC), ALU.mult)\
                    .then_inc(S["pool_early"], 1)
                pool.wait_ge(S["pool_early"], h + 1)
                pool.tensor_tensor(minv_t[:, :, :], minv_t[:, :, :], each(ident[:, :], NC), ALU.add)\
                    .then_inc(S["g_mt0"], 1)
                for l in range(2, LEVELS):
                    pool.wait_ge(S["g_m"], 6 * h + l - 1)
                    if l > 2:
                        pool.wait_ge(S["g_mt"], 6 * h + l - 2)
                    plain()
                    pool.memset(xx[l % 2][:, :, :], 0.0).then_inc(S["g_xz"], 1)
                for half in range(2):
                    c4 = slice(4 * half, 4 * half + 4)
                    pool.wait_ge(S["g_oms"], 2 * h + half + 1)
                    pool.tensor_tensor(sm[:, 6, c4], sm[:, 5, c4], minus_half[:, c4], ALU.pow).then_inc(S["g_ors"], 1)

            def mlstm(h, nxt):
                pool.wait_ge(S["head_done"], h + GH + 1)
                start_split(nxt)
                pool.wait_ge(S["unit_out"], units_before((MLSTM, h)) + 10)
                plain()
                pool.tensor_copy(qk[:, :, 1, :], raw[:, 0, PAST:].rearrange("p (c t) -> p c t", c=NC))\
                    .then_inc(S["m_qk"], 1)
                pool.tensor_copy(qk[:, :, 0, :], raw[:, 1, PAST:].rearrange("p (c t) -> p c t", c=NC))\
                    .then_inc(S["m_qk"], 1)
                pool.wait_ge(S["m_tab"], h + 1)
                pool.tensor_tensor(gu[:, :, :], each(upper[:, :], NC), over(ht[:, T_G, :], P), ALU.mult)\
                    .then_inc(S["m_gu"], 1)
                pool.wait_ge(S["m_sig"], 2 * h + 2)
                pool.tensor_tensor(sz[:, :], sz[:, :], raw[:, 4, PAST:], ALU.mult).then_inc(S["m_gate"], 1)
                pool.wait_ge(S["m_exp"], 2 * h + 2)
                pool.tensor_tensor(dd[:, 0:4, :, :].rearrange("p a b t -> p (a b) t"),
                                   dd[:, 4:8, :, :].rearrange("p a b t -> p (a b) t"),
                                   each(upper[:, :], NC), ALU.mult).then_inc(S["m_dd"], 1)
                for half in range(2):
                    c4 = slice(4 * half, 4 * half + 4)
                    pool.wait_ge(S["m_ms"], 2 * h + half + 1)
                    pool.tensor_tensor(sm[:, 6, c4], sm[:, 5, c4], minus_half[:, c4], ALU.pow).then_inc(S["m_rs"], 1)

            def memory(h):
                pool.wait_ge(S["head_done"], h + GH + MH + 1)
                plain()
                pool.tensor_copy(hkv[:, 0, :], kv[:, bass.ds(h, 1), :].rearrange("p a m -> p (a m)"))
                pool.tensor_copy(hkv[:, 1, :], kv[:, bass.ds(h + XH, 1), :].rearrange("p a m -> p (a m)"))\
                    .then_inc(S["x_kv"], 1)
                pool.wait_ge(S["unit_out"], units_before((MEM, h)) + 2)
                plain()
                pool.tensor_copy(vt[:, :], raw[:, 0, PAST:]).then_inc(S["x_q"], 1)

            with pool.Fori(0, GH - 1) as h:
                gdn(h, (GDN, h + 1))
            gdn(GH - 1, (MLSTM, 0))
            with pool.Fori(0, MH - 1) as h:
                mlstm(h, (MLSTM, h + 1))
            mlstm(MH - 1, (MEM, 0))
            with pool.Fori(0, XH) as h:
                memory(h)

            pool.wait_ge(S["head_done"], HEADS + 1)
            for i in range(KT):
                for j in range(2):
                    pool.wait_ge(S[f"o_load{j}"], 16 * (i + 1))
                    pool.tensor_copy(wo_hi[j][:, i, :], wo_raw[j][:, :]).then_inc(S[f"o_hi{j}"], 1)
            for t in range(NC):
                pool.wait_ge(S["o_ms"], t + 1)
                pool.tensor_tensor(sm[:, 1, 0:1], sm[:, 0, 0:1], minus_half[:, 0:1], ALU.pow).then_inc(S["o_rs"], 1)

        @block.scalar
        def _(act):
            def unit_copy(head, u, free):
                act.wait_ge(S["unit_done"], units_before(head) + u + 1)
                b, half = u // 2, u % 2
                if half == 0:
                    free(b)
                act.activation(raw[:, b, PAST + half * HALF:PAST + (half + 1) * HALF], ps[:, half, :], ACT.Copy)\
                    .then_inc(S["unit_out"], 1)

            def advance(nxt, st, upto, free, more=True):
                while (st[0] + 1) * UNIT <= upto:
                    u = st[0]
                    st[0] += 1
                    unit_copy(nxt, u, free)
                    slot = SLOTS[nxt[0]][u // 2]
                    if u % 2 and slot < 2 and more:
                        n = uses(slot, nxt, u // 2) + 1
                        act.wait_ge(w_loaded[slot], 16 * n)
                        act.activation(w_hi[slot][:, :, :], w_raw[slot][:, :, :], ACT.Copy).then_inc(w_hi_done[slot], 1)

            early = Steps(act, S["early_act"])
            for i in range(2 + NC + 1):
                if i < 2 + NC:
                    act.wait_ge(S[f"x_loaded{i % 2}"], 16 * (i // 2 + 1))
                    if i:
                        act.wait_ge(S["x_square"], i)
                    act.activation(mix[:, :], x_in[:, i % 2, :], ACT.Square, accum_out=ss_tiles[:, i:i + 1])\
                        .then_inc(S["x_square"], 1)
                if i >= 1:
                    j = i - 1
                    hi = (mem_hi[:, :, j * P:(j + 1) * P] if j < 2 else xn_hi[:, :, (j - 2) * P:(j - 1) * P])
                    for q in range(2):
                        act.wait_ge(S["x_turned"], 2 * j + q + 1)
                        act.activation(hi[:, 4 * q:4 * q + 4, :],
                                       ps[:, 4 + 2 * (j % 2) + q, :].rearrange("p (k t) -> p k t", k=4), ACT.Copy)\
                            .then_inc(S["x_hi"], 1)
                if 3 <= i:
                    b = i - 3
                    act.wait_ge(S["unit_done"], b + 1)
                    act.activation(kv[:, b, :], ps[:, b % 2, 0:N_MEM], ACT.Copy).then_inc(S["unit_out"], 1)
            act.sem_inc(S["mix_stored"], 16)
            act.preload_act_table_set("natural_log_exp_and_others")
            act.wait_ge(S["tiny"], 64)
            act.activation(gcol[R_GA:R_GA + GH, 2:3], gcol[R_GA:R_GA + GH, 2:3], ACT.Exp).then_inc(S["gate_exp"], 1)
            act.wait_ge(S["gate_m"], 1)
            for half in range(2):
                cols = slice(half * HALF, (half + 1) * HALF)
                act.wait_ge(S["unit_done"], 2 * XH + half + 1)
                act.activation(z_row[0:64, cols], ps[0:64, half, :], ACT.Identity, bias=gcol[0:64, 1:2],
                               scale=gcol[0:64, 0:1])
                act.activation(rows[64:96, cols], ps[64:96, half, :], ACT.Exp, scale=-1.0)
                act.activation(i_row[32:64, cols], ps[96:128, half, :], ACT.Copy).then_inc(S["unit_out"], 1)
            act.wait_ge(S["unit_out"], 2 * XH + 2)
            early.done(act.activation(e_row[0:64, :], z_row[0:64, :], ACT.Abs))
            act.activation(e_row[0:64, :], e_row[0:64, :], ACT.Exp, scale=-1.0).then_inc(S["gate_act"], 1)
            act.wait_ge(S["gate_rows"], 1)
            act.activation(l_row[0:64, :], u_row[0:64, :], ACT.Ln).then_inc(S["gate_act"], 1)
            st = [0]
            advance((GDN, 0), st, UNITS[GDN] * UNIT, lambda b: None)
            act.wait_ge(S["gate_tab"], 1)
            act.wait_ge(S["gate_turned"], 3)
            act.activation(tab[:, GH:, T_X, :].rearrange("p h c -> p c h"),
                           ps[:, 4:6, :].rearrange("p a (c r) -> p (a c) r", c=4)[:, :, R_MI:R_MI + MH], ACT.Exp)
            act.activation(guard[:, :, :].rearrange("p h c -> p c h"),
                           ps[:, 6, 0:NC * 32].rearrange("p (c r) -> p c r", c=NC)[:, :, 0:MH], ACT.Exp, scale=-1.0)\
                .then_inc(S["gate_exp"], 1)
            act.wait_ge(S["gate_sum"], 1)
            act.activation(tab[:, :, T_E:T_L + 1, :].rearrange("p h k c -> p k h c"),
                           ps[:, 7, 0:3 * 96].rearrange("p (k h c) -> p k h c", k=3, h=GH + MH), ACT.Exp)\
                .then_inc(S["gate_exp"], 1)

            dd_spare = flat(dd)[:, SEQ:].rearrange("p (c t) -> p c t", c=NC)

            def squares(ready, base, src, spare, c, out):
                act.wait_ge(ready, base + c + 1)
                act.activation(spare[:, c, :], src[:, c, :], ACT.Square, accum_out=sm[:, 8, c:c + 1]).then_inc(out, 1)

            def gdn(h, nxt):
                cum, st = plan(GDN, nxt and nxt[0]), [0]

                def free(b):
                    if b < 3:
                        act.wait_ge(S["g_conv"], 3 * h + b + 1)

                act.wait_ge(S["head_done"], h + 1)
                for b, (src, dst) in enumerate(((flat(pair)[:, 0:SEQ], qk[:, :, 1, :]), (flat(pair)[:, SEQ:], qk[:, :, 0, :]))):
                    act.wait_ge(S["g_conv"], 3 * h + b + 1)
                    act.activation(dst, src.rearrange("p (c t) -> p c t", c=NC), ACT.Silu).then_inc(S["g_silu"], 1)
                    act.wait_ge(S["g_silu"], 4 * h + b + 1)
                    act.activation(dd[:, :, 1 - b, :], dst, ACT.Square).then_inc(S["g_sq"], 1)
                    advance(nxt, st, min(2 * (b + 1) * UNIT, cum["sums"]), free)
                for half in range(2):
                    act.wait_ge(S["g_decay"], 2 * h + half + 1)
                    act.activation(xx[1][:, 4 * half:4 * half + 4, :],
                                   ps[:, 6 + half, :].rearrange("p (c t) -> p c t", c=4), ACT.Exp)\
                        .then_inc(S["g_exp"], 1)
                act.wait_ge(S["g_conv"], 3 * h + 3)
                act.activation(vt[:, :].rearrange("p (c t) -> p c t", c=NC), nv[:, :, :], ACT.Silu).then_inc(S["g_silu"], 1)
                act.wait_ge(S["unit_out"], units_before((GDN, h)) + 8)
                act.activation(sz[:, :], raw[:, 3, PAST:], ACT.Silu).then_inc(S["g_silu"], 1)
                for l in range(1, LEVELS):
                    advance(nxt, st, cum[f"b{l}"], free)
                for c in range(NC):
                    advance(nxt, st, cum[f"r{c}"], free)
                    if c:
                        act.wait_ge(S["g_qs"], 7 * h + c)
                        if c > 2:
                            act.wait_ge(S["g_o"], 8 * h + c - 1)
                        act.activation(carried[:, c % 2, 0:P], ps[:, 3, 0:P], ACT.Copy, scale=ht[:, T_E, c:c + 1])\
                            .then_inc(S["g_cq"], 1)
                        squares(S["g_o"], 8 * h, gu, xx[0], c - 1, S["g_osq"])
                squares(S["g_o"], 8 * h, gu, xx[0], NC - 1, S["g_osq"])
                advance(nxt, st, cum["end"], free)
                act.wait_ge(S["head_done"], h + 2)
                act.dma_start(mixed[bass.ds(h * P, P), :], mix[:, :]).then_inc(S["mix_stored"], 16)

            def mlstm(h, nxt):
                cum, st = plan(MLSTM, nxt and nxt[0]), [0]

                def free(b):
                    if b < 2:
                        act.wait_ge(S["m_qk"], 2 * h + b + 1)
                    elif b == 2:
                        act.wait_ge(S["m_v"], 2 * h + 2)
                    elif b == 4:
                        act.wait_ge(S["m_gate"], h + 1)

                act.wait_ge(S["head_done"], h + GH + 1)
                act.wait_ge(S["unit_out"], units_before((MLSTM, h)) + 10)
                act.activation(vt[:, :], raw[:, 3, PAST:], ACT.Sigmoid).then_inc(S["m_sig"], 1)
                act.activation(sz[:, :], raw[:, 4, PAST:], ACT.Sigmoid).then_inc(S["m_sig"], 1)
                advance(nxt, st, cum["decay"], free)
                for half in range(2):
                    act.wait_ge(S["m_decay"], 2 * h + half + 1)
                    act.activation(flat(dd)[:, SEQ + half * HALF:SEQ + (half + 1) * HALF], ps[:, 6 + half, :], ACT.Exp)\
                        .then_inc(S["m_exp"], 1)
                advance(nxt, st, cum["o"], free)
                for half in range(2):
                    act.wait_ge(S["m_o"], 2 * h + half + 1)
                    act.activation(flat(pair)[:, SEQ + half * HALF:SEQ + (half + 1) * HALF], ps[:, 2 + half, :], ACT.Copy)\
                        .then_inc(S["m_sg"], 1)
                for c in range(NC):
                    advance(nxt, st, cum[f"c{c}"], free)
                    if c:
                        act.wait_ge(S["m_qc"], 7 * h + c)
                        if c > 2:
                            act.wait_ge(S["m_nd"], 8 * h + c - 1)
                        act.activation(carried[:, c % 2, :], ps[:, 3, 0:P + 1], ACT.Copy, scale=ht[:, T_E, c:c + 1])\
                            .then_inc(S["m_cq"], 1)
                    if c == 5:
                        for i in range(4):
                            squares(S["m_h"], 8 * h, nv, dd_spare, i, S["m_hsq"])
                for i in range(4, NC):
                    squares(S["m_h"], 8 * h, nv, dd_spare, i, S["m_hsq"])
                advance(nxt, st, cum["end"], free)
                act.wait_ge(S["head_done"], h + GH + 2)
                act.dma_start(mixed[bass.ds(h * P + GW, P), :], mix[:, :]).then_inc(S["mix_stored"], 16)

            def memory(h, nxt, more):
                cum, st = plan(MEM, nxt and nxt[0]), [0]

                def free(b):
                    if b == 0:
                        act.wait_ge(S["x_q"], h + 1)

                act.wait_ge(S["head_done"], h + GH + MH + 1)
                act.wait_ge(S["unit_out"], units_before((MEM, h)) + 4)
                act.activation(sz[:, :], raw[:, 1, PAST:], ACT.Silu).then_inc(S["x_silu"], 1)
                if nxt is not None:
                    advance(nxt, st, cum["scores"], free, more)
                for c in range(NC):
                    act.wait_ge(S["x_sc"], 4 * h + c // 2 + 1)
                    act.wait_ge(S["x_nb"], 4 * h + c // 2 + 1)
                    act.activation(flat(dd)[:, c * N_MEM:(c + 1) * N_MEM], ps[:, 2 + c // 2, (c % 2) * N_MEM:(c % 2 + 1) * N_MEM],
                                   ACT.Exp, scale=SCALE, bias=sm[:, 1, c:c + 1], accum_out=sm[:, 2, c:c + 1])\
                        .then_inc(S["x_p"], 1)
                if nxt is not None:
                    advance(nxt, st, cum["probs"], free, more)
                for q in range(4):
                    act.wait_ge(S["x_pt"], 4 * h + q + 1)
                    act.activation(flat(pair)[:, q * HALF:(q + 1) * HALF], ps[:, 4 + q, :], ACT.Copy)\
                        .then_inc(S["x_ptc"], 1)
                if nxt is not None:
                    advance(nxt, st, cum["end"], free, more)
                act.wait_ge(S["head_done"], h + GH + MH + 2)
                act.dma_start(mixed[bass.ds(h * P + GW + MW, P), :], mix[:, :]).then_inc(S["mix_stored"], 16)

            with act.Fori(0, GH - 1) as h:
                gdn(h, (GDN, h + 1))
            gdn(GH - 1, (MLSTM, 0))
            with act.Fori(0, MH - 1) as h:
                mlstm(h, (MLSTM, h + 1))
            mlstm(MH - 1, (MEM, 0))
            with act.Fori(0, XH - 2) as h:
                memory(h, (MEM, h + 1), True)
            memory(XH - 2, (MEM, XH - 1), False)
            memory(XH - 1, None, False)

            act.wait_ge(S["mix_stored"], 16 * (HEADS + 1))
            for t in range(NC + 1):
                if t < NC:
                    act.wait_ge(S["o_mx"], 16 * (t + 1))
                    if t >= 2:
                        act.wait_ge(S["o_ps"], 2 * (t - 1))
                    act.activation(mx_hi[t % 2][:, :, :], mx_raw[:, :, :], ACT.Copy).then_inc(S["o_mhi"], 1)
                if t:
                    act.wait_ge(S["o_y"], 2 * t)
                    act.activation(y_sq[:, :], y[:, :], ACT.Square, accum_out=sm[:, 2, 0:1]).then_inc(S["o_sq"], 1)

        @block.vector
        def _(dve):
            def split_lo(slot, n):
                dve.wait_ge(w_hi_done[slot], n)
                dve.tensor_tensor(w_lo[slot][:, :, :], w_raw[slot][:, :, :], w_hi[slot][:, :, :].bitcast(F32),
                                  ALU.subtract).then_inc(w_split[slot], 1)

            def advance(nxt, st, upto, more=True):
                while (st[0] + 1) * UNIT <= upto:
                    u = st[0]
                    st[0] += 1
                    slot = SLOTS[nxt[0]][u // 2]
                    if u % 2 and slot < 2 and more:
                        split_lo(slot, uses(slot, nxt, u // 2) + 1)

            dve.wait_ge(S["grows"], 32)
            for i in range(2 + NC + 1):
                if i < 2 + NC:
                    if i >= 2:
                        dve.wait_ge(S["x_turned"], 2 * (i - 1))
                    dve.wait_ge(S["x_rstd"], i + 1)
                    dve.scalar_tensor_tensor(out=x_tok[:, i % 2, :], in0=x_in[:, i % 2, :],
                                             scalar=rstd_tiles[:, i:i + 1], in1=g_rows[:, 1 if i < 2 else 0, :],
                                             op0=ALU.mult, op1=ALU.mult).then_inc(S["x_scaled"], 1)
                if i >= 1:
                    j = i - 1
                    hi, lo = ((mem_hi, mem_lo) if j < 2 else (xn_hi, xn_lo))
                    cols = slice(j * P, (j + 1) * P) if j < 2 else slice((j - 2) * P, (j - 1) * P)
                    for q in range(2):
                        dve.wait_ge(S["x_hi"], 2 * j + q + 1)
                        dve.tensor_tensor(lo[:, 4 * q:4 * q + 4, cols],
                                          ps[:, 4 + 2 * (j % 2) + q, :].rearrange("p (k t) -> p k t", k=4),
                                          hi[:, 4 * q:4 * q + 4, cols].bitcast(F32), ALU.subtract)\
                            .then_inc(S["x_lo"], 1)
                if 1 <= i <= 2 * XH:
                    split_lo((i - 1) % 2, (i - 1) // 2 + 1)
            split_lo(2, 1)
            split_lo(0, KV_USES + 1)
            split_lo(1, KV_USES + 1)

            early = Steps(dve, S["early_dve"])
            dve.wait_ge(S["tiny"], 64)
            dve.wait_ge(S["gate_exp"], 1)
            dve.memset(gcol[0:32, 0:1], 1.0)
            dve.memset(gcol[32:64, 0:1], -1.0)
            dve.memset(gcol[32:64, 2:3], -1.0)
            dve.tensor_scalar(gcol[0:32, 2:3], gcol[0:32, 2:3], -1.0, None, ALU.mult)
            dve.tensor_scalar(gcol[32:64, 1:2], gcol[32:64, 1:2], -1.0, None, ALU.mult).then_inc(S["gate_m"], 1)
            dve.wait_ge(S["gate_act"], 1)
            dve.tensor_scalar(u_row[0:64, :], e_row[0:64, :], 1.0, None, ALU.add).then_inc(S["gate_rows"], 1)
            dve.wait_ge(S["gate_rows"], 1)
            early.done(dve.scalar_tensor_tensor(out=e_row[0:64, :], in0=u_row[0:64, :], scalar=1.0, in1=e_row[0:64, :],
                                                op0=ALU.subtract, op1=ALU.subtract))
            dve.wait_ge(S["gate_act"], 2)
            early.done(dve.tensor_tensor(l_row[0:64, :], l_row[0:64, :], e_row[0:64, :], ALU.subtract))
            early.done(dve.scalar_tensor_tensor(out=l_row[0:64, :], in0=z_row[0:64, :], scalar=0.0, in1=l_row[0:64, :],
                                                op0=ALU.max, op1=ALU.add))
            dve.tensor_scalar(i_row[32:64, :], i_row[32:64, :], gcol[32:64, 3:4], None, ALU.add)
            early.done(dve.tensor_scalar(rows[0:64, :], l_row[0:64, :], gcol[0:64, 2:3], None, ALU.mult))
            mh = slice(R_MF, R_MF + MH)
            early.done(dve.tensor_tensor_scan(m_row[mh, 1:SEQ + 1], rows[mh, :], i_row[mh, :], 0.0, ALU.add, ALU.max))
            early.done(dve.tensor_tensor(rows[mh, :], rows[mh, :], m_row[mh, 0:SEQ], ALU.add))
            dve.tensor_tensor(rows[mh, :], rows[mh, :], m_row[mh, 1:SEQ + 1], ALU.subtract)
            dve.tensor_tensor(rows[R_MI:R_MI + MH, :], i_row[mh, :], m_row[mh, 1:SEQ + 1], ALU.subtract)\
                .then_inc(S["gate_rows"], 1)
            st = [0]
            advance((GDN, 0), st, UNITS[GDN] * UNIT)
            dve.wait_ge(S["params_turned"], 1)
            dve.tensor_copy(params[:, 0:79], ps[:, 7, 0:79]).then_inc(S["params_out"], 1)
            dve.wait_ge(S["gate_turned"], 2)
            gates = ps[:, 4:6, :].rearrange("p a (c r) -> p (a c) r", c=4)
            dve.tensor_copy(tab[:, 0:GH, T_G, :].rearrange("p h c -> p c h"), gates[:, :, R_GA:R_GA + GH])
            dve.tensor_copy(tab[:, GH:, T_G, :].rearrange("p h c -> p c h"), gates[:, :, R_MF:R_MF + MH])
            eb = sm[:, 0:3, :].rearrange("p a b -> p (a b)")
            dve.tensor_scalar(eb.rearrange("p (h c) -> p c h", c=NC), gates[:, :, R_GB:R_GB + GH], 1.0, None, ALU.add)\
                .then_inc(S["gate_tab"], 1)
            dve.wait_ge(S["gate_tab"], 1)
            dve.reciprocal(tab[:, 0:GH, T_X, :], eb.rearrange("p (h c) -> p h c", c=NC))
            dve.wait_ge(S["gate_exp"], 2)
            dve.tensor_scalar(tab[:, GH:, T_X, :], tab[:, GH:, T_X, :], SCALE, None, ALU.mult)
            dve.wait_ge(S["gate_exp"], 3)
            dve.tensor_scalar(tab[:, :, T_NE, :], tab[:, :, T_E, :], -1.0, None, ALU.mult).then_inc(S["head_done"], 1)
            dve.wait_ge(S["head_done"], 1)

            def finish(H, ot, base, gain):
                dve.wait_ge(S["mix_stored"], 16 * (H + 1))
                for half in range(2):
                    cols = slice(half * HALF, (half + 1) * HALF)
                    dve.wait_ge(ot, base + half + 1)
                    if gain is None:
                        ins = dve.tensor_tensor(mix[:, cols], ps[:, 2 + half, :], sz[:, cols], ALU.mult)
                    else:
                        ins = dve.scalar_tensor_tensor(out=mix[:, cols], in0=ps[:, 2 + half, :], scalar=gain,
                                                       in1=sz[:, cols], op0=ALU.mult, op1=ALU.mult)
                ins.then_inc(S["head_done"], 1)

            GDN_STEPS = 18
            LAG = 12

            def gdn(h, nxt):
                cum, st = plan(GDN, nxt and nxt[0]), [0]
                step = Steps(dve, S["g_dve"], h * GDN_STEPS)

                def mean_square(half):
                    c4 = slice(4 * half, 4 * half + 4)
                    dve.wait_ge(S["g_osq"], 8 * h + 4 * half + 4)
                    step.done(dve.tensor_tensor(sm[:, 9, c4], sm[:, 9, c4], sm[:, 8, c4], ALU.mult))
                    dve.tensor_scalar(sm[:, 5, c4], sm[:, 9, c4], 1.0 / P, EPS, ALU.mult, ALU.add).then_inc(S["g_oms"], 1)

                def normalise(half):
                    c4 = slice(4 * half, 4 * half + 4)
                    dve.wait_ge(S["g_ors"], 2 * h + half + 1)
                    step.done(dve.tensor_tensor(sm[:, 10, c4], sm[:, 6, c4], sm[:, 7, c4], ALU.mult))
                    dve.tensor_tensor(fk[:, c4, :], gu[:, c4, :], over(sm[:, 10, c4], P), ALU.mult).then_inc(S["g_og"], 1)

                dve.wait_ge(S["head_done"], h + 1)
                dve.tensor_copy(ht[:, :, :], tab[:, bass.ds(h, 1), :, :].rearrange("p a k c -> p (a k) c"))\
                    .then_inc(S["g_tab"], 1)
                step.done(dve.tensor_copy(hconv[:, :], params[:, 0:72].rearrange("p (g h) -> p g h", h=GH)[:, :, bass.ds(h, 1)]
                                          .rearrange("p g a -> p (g a)")))
                dve.wait_ge(S["g_tab"], h + 1)
                for b, dst in enumerate((flat(pair)[:, 0:SEQ], flat(pair)[:, SEQ:],
                                         nv[:, :, :].rearrange("p c t -> p (c t)"))):
                    dve.wait_ge(S["unit_out"], units_before((GDN, h)) + 2 * b + 2)
                    step.done(dve.tensor_scalar(dst, raw[:, b, 0:SEQ], hconv[:, b:b + 1], None, ALU.mult))
                    for tap in range(1, 4):
                        ins = dve.scalar_tensor_tensor(out=dst, in0=raw[:, b, tap:tap + SEQ],
                                                       scalar=hconv[:, 3 * tap + b:3 * tap + b + 1], in1=dst,
                                                       op0=ALU.mult, op1=ALU.add)
                        if tap < 3:
                            step.done(ins)
                    ins.then_inc(S["g_conv"], 1)
                if nxt[0] == MLSTM:
                    split_lo(2, uses(2, nxt, 2))
                advance(nxt, st, cum["sums"])
                dve.wait_ge(S["g_ss"], h + 1)
                dve.tensor_scalar(sm[:, 0, :], ps[:, 2, 0:16], EPS, None, ALU.add).then_inc(S["g_sse"], 1)
                for half in range(2):
                    c4 = slice(4 * half, 4 * half + 4)
                    dve.wait_ge(S["g_exp"], 2 * h + half + 1)
                    step.done(dve.tensor_tensor(dd[:, c4, 1, :], xx[1][:, c4, :], each(upper[:, :], 4), ALU.mult))
                dve.wait_ge(S["g_rk"], h + 1)
                root = sm[:, 1, :].rearrange("p (c two) -> p c two", two=2)
                sums = sm[:, 0, :].rearrange("p (c two) -> p c two", two=2)
                dve.tensor_tensor(sm[:, 4, 0:NC], sums[:, :, 0], root[:, :, 0], ALU.mult)
                dve.tensor_scalar(sm[:, 7, 0:NC], root[:, :, 1], SCALE, None, ALU.mult)
                step.done(dve.tensor_tensor(sm[:, 3, 0:NC], root[:, :, 0], root[:, :, 0], ALU.mult))
                dve.tensor_tensor(sm[:, 2, 0:NC], sm[:, 3, 0:NC], ht[:, T_X, :], ALU.mult).then_inc(S["g_w"], 1)
                step.done(dve.tensor_tensor(sm[:, 9, 0:NC], sm[:, 7, 0:NC], sm[:, 7, 0:NC], ALU.mult))
                dve.wait_ge(S["g_w"], h + 1)
                dve.tensor_tensor(dd[:, :, 0, :], dd[:, :, 1, :], over(sm[:, 2, 0:NC], P), ALU.mult).then_inc(S["g_dd"], 1)
                dve.wait_ge(S["g_dd"], h + 1)
                for i in range(4):
                    dve.wait_ge(S["g_kq"], 4 * h + i + 1)
                    dve.tensor_tensor(pair[:, 2 * i:2 * i + 2, :, :].rearrange("p c two t -> p (c two t)"), ps[:, 2 + i, :],
                                      dd[:, 2 * i:2 * i + 2, :, :].rearrange("p c two t -> p (c two t)"), ALU.mult)\
                        .then_inc(S["g_pair"], 1)
                for half in range(2):
                    c4 = slice(4 * half, 4 * half + 4)
                    dve.wait_ge(S["g_kt"], 2 * h + half + 1)
                    dve.tensor_tensor(fk[:, c4, :], ps[:, 6 + half, :].rearrange("p (c t) -> p c t", c=4),
                                      over(ht[:, T_F, c4], P), ALU.mult).then_inc(S["g_fk"], 1)
                for half in range(2):
                    c4 = slice(4 * half, 4 * half + 4)
                    dve.wait_ge(S["g_vt"], 2 * h + half + 1)
                    dve.tensor_tensor(nv[:, c4, :], ps[:, 2 + half, :].rearrange("p (c t) -> p c t", c=4),
                                      over(sm[:, 4, c4], P), ALU.mult).then_inc(S["g_nv"], 1)
                for l in range(LEVELS):
                    if l:
                        advance(nxt, st, cum[f"b{l}"] - LAG)
                    b = 1 << l
                    dve.wait_ge(S["g_a"], 7 * h + l + 1)
                    dve.wait_ge(S["g_xz"], 7 * h + l + 1)
                    x_low = halves(xx[l % 2], l)[0]
                    mask = level_mask[:, l, :].rearrange("p (n b) -> p n b", b=b).unsqueeze(1)\
                        .broadcast_to([P, NC, 64 // b, b])
                    dve.tensor_tensor(x_low, packed(4, l), mask, ALU.mult).then_inc(S["g_x"], 1)
                    m_low, mt_high = halves(minv, l)[0], halves(minv_t, l)[1]
                    if l == 0:
                        dve.wait_ge(S["g_x"], 7 * h + 1)
                        dve.wait_ge(S["g_m0"], h + 1)
                        dve.tensor_tensor(m_low, x_low, m_low, ALU.add).then_inc(S["g_m"], 1)
                        continue
                    if l < LEVELS - 1:
                        dve.wait_ge(S["g_b"], 5 * h + l)
                        dve.tensor_tensor(m_low, packed(5, l), m_low, ALU.add).then_inc(S["g_m"], 1)
                    dve.wait_ge(S["g_c"], 6 * h + l)
                    dve.tensor_tensor(mt_high, packed(6, l), mt_high, ALU.add).then_inc(S["g_mt"], 1)
                for c in range(NC):
                    advance(nxt, st, cum[f"r{c}"] - LAG)
                    if c:
                        dve.wait_ge(S["g_ks"], 7 * h + c)
                        dve.scalar_tensor_tensor(out=rhs[:, c % 2, :], in0=ps[:, 2, 0:P], scalar=ht[:, T_NE, c:c + 1],
                                                 in1=nv[:, c, :], op0=ALU.mult, op1=ALU.add).then_inc(S["g_r"], 1)
                    dve.wait_ge(S["g_y"], 8 * h + c + 1)
                    dve.tensor_scalar(zed[:, c % 2, :], ps[:, 4, 0:P], sm[:, 2, c:c + 1], None, ALU.mult)\
                        .then_inc(S["g_z"], 1)
                    if c < NC - 1:
                        dve.wait_ge(S["g_up"], 7 * h + c + 1)
                        if c == 0:
                            ins = dve.tensor_copy(state[:, 0:P], ps[:, 5, 0:P])
                        else:
                            ins = dve.scalar_tensor_tensor(out=state[:, 0:P], in0=state[:, 0:P], scalar=ht[:, T_L, c:c + 1],
                                                           in1=ps[:, 5, 0:P], op0=ALU.mult, op1=ALU.add)
                        ins.then_inc(S["g_s"], 1)
                    dve.wait_ge(S["g_att"], 8 * h + c + 1)
                    if c == 0:
                        ins = dve.tensor_copy(gu[:, 0, :], ps[:, 6, 0:P])
                    else:
                        dve.wait_ge(S["g_cq"], 7 * h + c)
                        ins = dve.tensor_tensor(gu[:, c, :], carried[:, c % 2, 0:P], ps[:, 6 + c % 2, 0:P], ALU.add)
                    ins.then_inc(S["g_o"], 1)
                    if c == 5:
                        mean_square(0)
                    if c == 6:
                        normalise(0)
                mean_square(1)
                normalise(1)
                assert step.n == GDN_STEPS, step.n
                finish(h, S["g_ot"], 2 * h, params[:, 72:73])
                advance(nxt, st, cum["end"])

            MLSTM_STEPS = 12

            def mlstm(h, nxt):
                cum, st = plan(MLSTM, nxt and nxt[0]), [0]
                step = Steps(dve, S["m_dve"], h * MLSTM_STEPS)
                sg = flat(pair)[:, SEQ:].rearrange("p (c t) -> p c t", c=NC)

                def gate(half):
                    c4 = slice(4 * half, 4 * half + 4)
                    dve.wait_ge(S["m_nd"], 8 * h + 4 * half + 4)
                    den = num_den[:, c4, P]
                    step.done(dve.scalar_tensor_tensor(out=sm[:, 0, c4], in0=den, scalar=-1.0, in1=den,
                                                       op0=ALU.mult, op1=ALU.max))
                    dve.wait_ge(S["m_sg"], 2 * h + 2)
                    for c in range(4 * half, 4 * half + 4):
                        dve.tensor_tensor(nv[:, c, :], num_den[:, c, 0:P], sg[:, c, :], ALU.mult).then_inc(S["m_h"], 1)
                    step.done(dve.tensor_tensor(sm[:, 1, c4], sm[:, 0, c4], hguard[:, c4], ALU.max))
                    step.done(dve.reciprocal(sm[:, 7, c4], sm[:, 1, c4]))
                    step.done(dve.tensor_tensor(sm[:, 9, c4], sm[:, 7, c4], sm[:, 7, c4], ALU.mult))

                def mean_square(half):
                    c4 = slice(4 * half, 4 * half + 4)
                    dve.wait_ge(S["m_hsq"], 8 * h + 4 * half + 4)
                    step.done(dve.tensor_tensor(sm[:, 9, c4], sm[:, 9, c4], sm[:, 8, c4], ALU.mult))
                    dve.tensor_scalar(sm[:, 5, c4], sm[:, 9, c4], 1.0 / P, EPS, ALU.mult, ALU.add).then_inc(S["m_ms"], 1)

                def normalise(half):
                    c4 = slice(4 * half, 4 * half + 4)
                    dve.wait_ge(S["m_rs"], 2 * h + half + 1)
                    step.done(dve.tensor_tensor(sm[:, 10, c4], sm[:, 6, c4], sm[:, 7, c4], ALU.mult))
                    dve.tensor_tensor(fk[:, c4, :], nv[:, c4, :], over(sm[:, 10, c4], P), ALU.mult).then_inc(S["m_og"], 1)

                dve.wait_ge(S["head_done"], h + GH + 1)
                dve.tensor_copy(hguard[:, :], guard[:, bass.ds(h, 1), :].rearrange("p a c -> p (a c)"))
                dve.tensor_copy(hnorm[:, :], params[:, bass.ds(h + 73, 1)])
                dve.tensor_copy(ht[:, :, :], tab[:, bass.ds(h + GH, 1), :, :].rearrange("p a k c -> p (a k) c"))\
                    .then_inc(S["m_tab"], 1)
                dve.wait_ge(S["m_tab"], h + 1)
                for half in range(2):
                    c4 = slice(4 * half, 4 * half + 4)
                    dve.wait_ge(S["m_v"], 2 * h + half + 1)
                    dve.tensor_tensor(v_ext[:, c4, 0:P], ps[:, 2 + half, :].rearrange("p (c t) -> p c t", c=4),
                                      over(ht[:, T_X, c4], P), ALU.mult).then_inc(S["m_ve"], 1)
                dve.tensor_copy(v_ext[:, :, P], ht[:, T_X, :]).then_inc(S["m_ve"], 1)
                if nxt[0] == MLSTM:
                    split_lo(2, uses(2, nxt, 2))
                advance(nxt, st, cum["pairs"] - LAG)
                dve.wait_ge(S["m_dd"], h + 1)
                for half in range(2):
                    dve.wait_ge(S["m_pair"], 2 * h + half + 1)
                    dve.tensor_tensor(flat(pair)[:, half * HALF:(half + 1) * HALF], ps[:, 4 + half, :],
                                      flat(dd)[:, half * HALF:(half + 1) * HALF], ALU.mult).then_inc(S["m_pm"], 1)
                for half in range(2):
                    c4 = slice(4 * half, 4 * half + 4)
                    dve.wait_ge(S["m_k"], 2 * h + half + 1)
                    dve.tensor_tensor(fk[:, c4, :], ps[:, 6 + half, :].rearrange("p (c t) -> p c t", c=4),
                                      over(ht[:, T_F, c4], P), ALU.mult).then_inc(S["m_fk"], 1)
                for c in range(NC):
                    advance(nxt, st, cum[f"c{c}"] - LAG)
                    if c < NC - 1:
                        dve.wait_ge(S["m_up"], 7 * h + c + 1)
                        if c == 0:
                            ins = dve.tensor_copy(state[:, :], ps[:, 5, 0:P + 1])
                        else:
                            ins = dve.scalar_tensor_tensor(out=state[:, :], in0=state[:, :], scalar=ht[:, T_L, c:c + 1],
                                                           in1=ps[:, 5, 0:P + 1], op0=ALU.mult, op1=ALU.add)
                        ins.then_inc(S["m_s"], 1)
                    dve.wait_ge(S["m_pv"], 8 * h + c + 1)
                    if c == 0:
                        ins = dve.tensor_copy(num_den[:, 0, :], ps[:, 6, 0:P + 1])
                    else:
                        dve.wait_ge(S["m_cq"], 7 * h + c)
                        ins = dve.tensor_tensor(num_den[:, c, :], carried[:, c % 2, :], ps[:, 6 + c % 2, 0:P + 1], ALU.add)
                    ins.then_inc(S["m_nd"], 1)
                    if c == 4:
                        gate(0)
                    if c == 5:
                        mean_square(0)
                    if c == 6:
                        normalise(0)
                gate(1)
                mean_square(1)
                normalise(1)
                assert step.n == MLSTM_STEPS, step.n
                finish(h + GH, S["m_ot"], 2 * h, hnorm[:, 0:1])
                advance(nxt, st, cum["end"])

            MEM_STEPS = 5

            def memory(h, nxt, more):
                cum, st = plan(MEM, nxt and nxt[0]), [0]
                step = Steps(dve, S["x_dve"], h * MEM_STEPS)
                dve.wait_ge(S["x_v"], h + 1)
                dve.tensor_copy(vm[:, :, :].rearrange("p a t -> p (a t)"), ps[:, 2, 0:2 * P]).then_inc(S["x_vm"], 1)
                for i in range(4):
                    dve.wait_ge(S["x_sc"], 4 * h + i + 1)
                    step.done(dve.tensor_reduce(sm[:, 0, 2 * i:2 * i + 2],
                                                ps[:, 2 + i, :].rearrange("p (c m) -> p c m", c=2), AX.X, ALU.max))
                    dve.tensor_scalar(sm[:, 1, 2 * i:2 * i + 2], sm[:, 0, 2 * i:2 * i + 2], -SCALE, None, ALU.mult)\
                        .then_inc(S["x_nb"], 1)
                if nxt is not None:
                    advance(nxt, st, cum["probs"], more)
                dve.wait_ge(S["x_p"], 8 * h + 8)
                step.done(dve.reciprocal(sm[:, 3, 0:NC], sm[:, 2, 0:NC]))
                probs = flat(dd).rearrange("p (c m) -> p c m", c=NC)
                dve.tensor_tensor(probs, probs, over(sm[:, 3, 0:NC], N_MEM), ALU.mult).then_inc(S["x_pn"], 1)
                assert step.n == MEM_STEPS, step.n
                finish(h + GH + MH, S["x_o"], 2 * h, None)
                if nxt is not None:
                    advance(nxt, st, cum["end"], more)

            with dve.Fori(0, GH - 1) as h:
                gdn(h, (GDN, h + 1))
            gdn(GH - 1, (MLSTM, 0))
            with dve.Fori(0, MH - 1) as h:
                mlstm(h, (MLSTM, h + 1))
            mlstm(MH - 1, (MEM, 0))
            with dve.Fori(0, XH - 2) as h:
                memory(h, (MEM, h + 1), True)
            memory(XH - 2, (MEM, XH - 1), False)
            memory(XH - 1, None, False)

            for i in range(KT):
                for j in range(2):
                    dve.wait_ge(S[f"o_hi{j}"], i + 1)
                    dve.tensor_tensor(wo_lo[j][:, i, :], wo_raw[j][:, :], wo_hi[j][:, i, :].bitcast(F32), ALU.subtract)\
                        .then_inc(S[f"o_lo{j}"], 1)
                if i == 0:
                    dve.wait_ge(S["o_mhi"], 1)
                    dve.tensor_tensor(mx_lo[0][:, :, :], mx_raw[:, :, :], mx_hi[0][:, :, :].bitcast(F32), ALU.subtract)\
                        .then_inc(S["o_mlo"], 1)
            dve.wait_ge(S["o_fg"], 16)
            for t in range(1, NC + 1):
                if t < NC:
                    dve.wait_ge(S["o_mhi"], t + 1)
                    dve.tensor_tensor(mx_lo[t % 2][:, :, :], mx_raw[:, :, :], mx_hi[t % 2][:, :, :].bitcast(F32),
                                      ALU.subtract).then_inc(S["o_mlo"], 1)
                s = t - 1
                dve.wait_ge(S["o_x"], 16 * (s + 1))
                if s:
                    dve.wait_ge(S["o_st"], 16 * s)
                for half in range(2):
                    cols = slice(half * HALF, (half + 1) * HALF)
                    dve.wait_ge(S["o_ps"], 2 * s + half + 1)
                    dve.tensor_tensor(y[:, cols], ps[:, 2 + 2 * (s % 2) + half, :], x_t[:, cols], ALU.add)\
                        .then_inc(S["o_y"], 1)
                dve.wait_ge(S["o_sq"], s + 1)
                dve.tensor_scalar(sm[:, 0, 0:1], sm[:, 2, 0:1], 1.0 / D_MODEL, EPS, ALU.mult, ALU.add)\
                    .then_inc(S["o_ms"], 1)
                dve.wait_ge(S["o_rs"], s + 1)
                dve.scalar_tensor_tensor(out=y[:, :], in0=y[:, :], scalar=sm[:, 1, 0:1], in1=fg_row[:, :],
                                         op0=ALU.mult, op1=ALU.mult).then_inc(S["o_out"], 1)

        @block.tensor
        def _(pe):
            def products(slot, xh, xl, cols, k, term):
                w = (w_hi, w_hi, w_lo)[term][slot]
                v = (xh, xl, xh)[term]
                return w[:, k, :], v[:, k, cols]

            def project(nxt, st, upto):
                kind = nxt[0]
                while st[0] < upto:
                    u, i = divmod(st[0], UNIT)
                    st[0] += 1
                    slot, half = SLOTS[kind][u // 2], u % 2
                    if i == 0:
                        if half == 0:
                            pe.wait_ge(w_split[slot], uses(slot, nxt, u // 2))
                        pe.wait_ge(S["unit_out"], units_before(nxt) + u - 1)
                    k, term = divmod(i, TERMS)
                    w, v = products(slot, xn_hi, xn_lo, slice(half * HALF, (half + 1) * HALF), k, term)
                    mm = pe.matmul(ps[:, half, :], w, v, start=(i == 0), stop=(i == UNIT - 1))
                    if i == UNIT - 1:
                        mm.then_inc(S["unit_done"], 1)

            pe.wait_ge(S["consts"], 1)
            for i in range(2 + NC):
                if i >= 2:
                    pe.wait_ge(S["x_lo"], 2 * (i - 1))
                pe.wait_ge(S["x_scaled"], i + 1)
                for q in range(2):
                    for k in range(4):
                        mm = pe.transpose(ps[:, 4 + 2 * (i % 2) + q, k * P:(k + 1) * P],
                                          x_tok[:, i % 2, (4 * q + k) * P:(4 * q + k + 1) * P], ident[:, :])
                    mm.then_inc(S["x_turned"], 1)
                if i >= 2:
                    b = i - 2
                    pe.wait_ge(w_split[b % 2], b // 2 + 1)
                    if b == 0:
                        pe.wait_ge(S["x_lo"], 4)
                    if b >= 2:
                        pe.wait_ge(S["unit_out"], b - 1)
                    for j in range(UNIT):
                        w, v = products(b % 2, mem_hi, mem_lo, slice(0, N_MEM), *divmod(j, TERMS))
                        mm = pe.matmul(ps[:, b % 2, 0:N_MEM], w, v, start=(j == 0), stop=(j == UNIT - 1))
                    mm.then_inc(S["unit_done"], 1)
            pe.wait_ge(w_split[2], 1)
            pe.wait_ge(S["x_lo"], 2 * (2 + NC))
            for half in range(2):
                pe.wait_ge(S["unit_out"], 2 * XH - 1 + half)
                for j in range(UNIT):
                    w, v = products(2, xn_hi, xn_lo, slice(half * HALF, (half + 1) * HALF), *divmod(j, TERMS))
                    mm = pe.matmul(ps[:, half, :], w, v, start=(j == 0), stop=(j == UNIT - 1))
                mm.then_inc(S["unit_done"], 1)
            pe.wait_ge(S["rowz_loaded"], 96)
            pe.transpose(ps[:, 7, 0:79], param_rows[0:79, :], ident[0:79, 0:79]).then_inc(S["params_turned"], 1)
            project((GDN, 0), [0], UNITS[GDN] * UNIT)
            pe.wait_ge(S["gate_rows"], 2)
            for half in range(2):
                for c in range(4 * half, 4 * half + 4):
                    mm = pe.transpose(ps[:, 4 + half, (c % 4) * P:(c % 4 + 1) * P], rows[:, c * P:(c + 1) * P], ident[:, :])
                mm.then_inc(S["gate_turned"], 1)
            for c in range(NC):
                mm = pe.transpose(ps[:, 6, c * 32:(c + 1) * 32], m_row[32:64, 1 + c * P:1 + (c + 1) * P], ident[32:64, 32:64])
            mm.then_inc(S["gate_turned"], 1)
            pe.wait_ge(S["gate_tab"], 1)
            pe.wait_ge(S["params_out"], 1)
            for i, lhs in enumerate((upper, later, ones)):
                mm = pe.matmul(ps[:, 7, i * 96:(i + 1) * 96], lhs[:, :], tab[:, :, T_G, :], start=(i == 0), stop=(i == 2),
                               skip_group_check=True)
            mm.then_inc(S["gate_sum"], 1)

            def decay(gu_ready, out):
                pe.wait_ge(*gu_ready)
                for half in range(2):
                    pe.matmul(ps[:, 6 + half, :], later[:, :],
                              gu[:, 4 * half:4 * half + 4, :].rearrange("p c t -> p (c t)"), start=True, stop=True)\
                        .then_inc(out, 1)

            def turn(og, h, ot):
                for half in range(2):
                    pe.wait_ge(og, 2 * h + half + 1)
                    for c in range(4 * half, 4 * half + 4):
                        mm = pe.transpose(ps[:, 2 + half, (c % 4) * P:(c % 4 + 1) * P], fk[:, c, :], ident[:, :])
                    mm.then_inc(ot, 1)

            def gdn(h, nxt):
                cum, st = plan(GDN, nxt and nxt[0]), [0]
                sq = dd
                project(nxt, st, cum["decay"])
                decay((S["g_gu"], h + 1), S["g_decay"])
                project(nxt, st, cum["sums"])
                pe.wait_ge(S["g_sq"], 2 * h + 2)
                for c in range(NC):
                    for r in range(2):
                        mm = pe.matmul(ps[:, 2, 2 * c + r:2 * c + r + 1], sq[:, c, r, :], ones[:, 0:1],
                                       start=(c == 0 and r == 0), stop=(c == NC - 1 and r == 1), skip_group_check=True)
                mm.then_inc(S["g_ss"], 1)
                project(nxt, st, cum["pairs"])
                pe.wait_ge(S["g_sse"], h + 1)
                for i in range(4):
                    for c in (2 * i, 2 * i + 1):
                        mm = pe.matmul(ps[:, 2 + i, (c % 2) * 2 * P:(c % 2 + 1) * 2 * P], qk[:, c, 0, :],
                                       qk[:, c, :, :].rearrange("p two t -> p (two t)"), start=(c % 2 == 0), stop=(c % 2 == 1),
                                       skip_group_check=True)
                    mm.then_inc(S["g_kq"], 1)
                for half in range(2):
                    pe.wait_ge(S["g_exp"], 2 * h + half + 1)
                    for c in range(4 * half, 4 * half + 4):
                        mm = pe.transpose(ps[:, 6 + half, (c % 4) * P:(c % 4 + 1) * P], qk[:, c, 0, :], ident[:, :])
                    mm.then_inc(S["g_kt"], 1)
                pe.wait_ge(S["g_silu"], 4 * h + 3)
                for half in range(2):
                    pe.wait_ge(S["g_pair"], 4 * h + half + 1)
                    for c in range(4 * half, 4 * half + 4):
                        mm = pe.transpose(ps[:, 2 + half, (c % 4) * P:(c % 4 + 1) * P], vt[:, c * P:(c + 1) * P], ident[:, :])
                    mm.then_inc(S["g_vt"], 1)
                for l in range(LEVELS):
                    project(nxt, st, cum[f"a{l}"])
                    if l == 0:
                        pe.wait_ge(S["g_pair"], 4 * h + 4)
                    else:
                        pe.wait_ge(S["g_m"], 6 * h + l)
                    for c in range(NC):
                        low = (ident[:, :].rearrange("p (n two b) -> p n two b", two=2, b=1)[:, :, 0, :] if l == 0
                               else halves_of(minv, c, l)[0])
                        mm = pe.matmul(ps[:, 4, c * 64:(c + 1) * 64], pair[:, c, 0, :], low,
                                       start=(c == 0), stop=(c == NC - 1), skip_group_check=True)
                    mm.then_inc(S["g_a"], 1)
                    if l == 0:
                        continue
                    project(nxt, st, cum[f"b{l}"])
                    pe.wait_ge(S["g_x"], 7 * h + l + 1)
                    if l == 1:
                        pe.wait_ge(S["g_mt0"], h + 1)
                        pe.wait_ge(S["g_fk"], 2 * h + 2)
                    else:
                        pe.wait_ge(S["g_mt"], 6 * h + l - 1)
                    if l < LEVELS - 1:
                        for c in range(NC):
                            mm = pe.matmul(ps[:, 5, c * 64:(c + 1) * 64], minv_t[:, c, :], halves_of(xx[l % 2], c, l)[0],
                                           start=(c == 0), stop=(c == NC - 1), skip_group_check=True)
                        mm.then_inc(S["g_b"], 1)
                    for c in range(NC):
                        mm = pe.matmul(ps[:, 6, c * 64:(c + 1) * 64], xx[l % 2][:, c, :], halves_of(minv_t, c, l)[1],
                                       start=(c == 0), stop=(c == NC - 1), skip_group_check=True)
                    mm.then_inc(S["g_c"], 1)
                for c in range(NC):
                    project(nxt, st, cum[f"r{c}"])
                    if c:
                        pe.wait_ge(S["g_s"], 7 * h + c)
                        pe.matmul(ps[:, 2, 0:P], qk[:, c, 0, :], state[:, 0:P], start=True, stop=True).then_inc(S["g_ks"], 1)
                        if c > 1:
                            pe.wait_ge(S["g_cq"], 7 * h + c - 1)
                        pe.matmul(ps[:, 3, 0:P], qk[:, c, 1, :], state[:, 0:P], start=True, stop=True).then_inc(S["g_qs"], 1)
                    project(nxt, st, cum[f"y{c}"])
                    if c == 0:
                        pe.wait_ge(S["g_mt"], 6 * h + 6)
                        pe.wait_ge(S["g_nv"], 2 * h + 2)
                    else:
                        pe.wait_ge(S["g_r"], 7 * h + c)
                    pe.matmul(ps[:, 4, 0:P], minv_t[:, c, :], nv[:, 0, :] if c == 0 else rhs[:, c % 2, :],
                              start=True, stop=True).then_inc(S["g_y"], 1)
                    project(nxt, st, cum[f"s{c}"])
                    pe.wait_ge(S["g_z"], 8 * h + c + 1)
                    if c < NC - 1:
                        pe.matmul(ps[:, 5, 0:P], fk[:, c, :], zed[:, c % 2, :], start=True, stop=True).then_inc(S["g_up"], 1)
                    if c >= 2:
                        pe.wait_ge(S["g_o"], 8 * h + c - 1)
                    pe.matmul(ps[:, 6 + c % 2, 0:P], pair[:, c, 1, :], zed[:, c % 2, :], start=True, stop=True)\
                        .then_inc(S["g_att"], 1)
                project(nxt, st, cum["turn"])
                turn(S["g_og"], h, S["g_ot"])
                project(nxt, st, cum["end"])

            def mlstm(h, nxt):
                cum, st = plan(MLSTM, nxt and nxt[0]), [0]
                project(nxt, st, cum["v"])
                pe.wait_ge(S["head_done"], h + GH + 1)
                pe.wait_ge(S["unit_out"], units_before((MLSTM, h)) + 6)
                for half in range(2):
                    for c in range(4 * half, 4 * half + 4):
                        mm = pe.transpose(ps[:, 2 + half, (c % 4) * P:(c % 4 + 1) * P],
                                          raw[:, 2, PAST + c * P:PAST + (c + 1) * P], ident[:, :])
                    mm.then_inc(S["m_v"], 1)
                project(nxt, st, cum["decay"])
                decay((S["m_gu"], h + 1), S["m_decay"])
                project(nxt, st, cum["pairs"])
                pe.wait_ge(S["m_qk"], 2 * h + 2)
                for half in range(2):
                    for c in range(4 * half, 4 * half + 4):
                        mm = pe.matmul(ps[:, 4 + half, (c % 4) * P:(c % 4 + 1) * P], qk[:, c, 0, :], qk[:, c, 1, :],
                                       start=(c % 4 == 0), stop=(c % 4 == 3), skip_group_check=True)
                    mm.then_inc(S["m_pair"], 1)
                project(nxt, st, cum["k"])
                for half in range(2):
                    pe.wait_ge(S["m_exp"], 2 * h + half + 1)
                    for c in range(4 * half, 4 * half + 4):
                        mm = pe.transpose(ps[:, 6 + half, (c % 4) * P:(c % 4 + 1) * P], qk[:, c, 0, :], ident[:, :])
                    mm.then_inc(S["m_k"], 1)
                project(nxt, st, cum["o"])
                pe.wait_ge(S["m_sig"], 2 * h + 1)
                for half in range(2):
                    pe.wait_ge(S["m_ve"], 3 * h + half + 1)
                    for c in range(4 * half, 4 * half + 4):
                        mm = pe.transpose(ps[:, 2 + half, (c % 4) * P:(c % 4 + 1) * P], vt[:, c * P:(c + 1) * P], ident[:, :])
                    mm.then_inc(S["m_o"], 1)
                pe.wait_ge(S["m_fk"], 2 * h + 2)
                pe.wait_ge(S["m_sg"], 2 * h + 2)
                pe.wait_ge(S["m_ve"], 3 * h + 3)
                pe.wait_ge(S["m_pm"], 2 * h + 2)
                for c in range(NC):
                    project(nxt, st, cum[f"c{c}"])
                    if c:
                        pe.wait_ge(S["m_s"], 7 * h + c)
                        if c > 1:
                            pe.wait_ge(S["m_cq"], 7 * h + c - 1)
                        pe.matmul(ps[:, 3, 0:P + 1], qk[:, c, 1, :], state[:, :], start=True, stop=True)\
                            .then_inc(S["m_qc"], 1)
                    if c < NC - 1:
                        pe.matmul(ps[:, 5, 0:P + 1], fk[:, c, :], v_ext[:, c, :], start=True, stop=True)\
                            .then_inc(S["m_up"], 1)
                    if c >= 2:
                        pe.wait_ge(S["m_nd"], 8 * h + c - 1)
                    pe.matmul(ps[:, 6 + c % 2, 0:P + 1], flat(pair)[:, c * P:(c + 1) * P], v_ext[:, c, :],
                              start=True, stop=True).then_inc(S["m_pv"], 1)
                project(nxt, st, cum["turn"])
                turn(S["m_og"], h, S["m_ot"])
                project(nxt, st, cum["end"])

            def memory(h, nxt):
                cum, st = plan(MEM, nxt and nxt[0]), [0]
                if nxt is not None:
                    project(nxt, st, cum["v"])
                pe.wait_ge(S["x_kv"], h + 1)
                for m in range(2):
                    mm = pe.transpose(ps[:, 2, m * P:(m + 1) * P], hkv[:, 1, m * P:(m + 1) * P], ident[:, :])
                mm.then_inc(S["x_v"], 1)
                if nxt is not None:
                    project(nxt, st, cum["scores"])
                pe.wait_ge(S["x_vm"], h + 1)
                pe.wait_ge(S["x_q"], h + 1)
                for c in range(NC):
                    mm = pe.matmul(ps[:, 2 + c // 2, (c % 2) * N_MEM:(c % 2 + 1) * N_MEM], vt[:, c * P:(c + 1) * P],
                                   hkv[:, 0, :], start=(c % 2 == 0), stop=(c % 2 == 1), skip_group_check=True)
                    if c % 2:
                        mm.then_inc(S["x_sc"], 1)
                if nxt is not None:
                    project(nxt, st, cum["probs"])
                pe.wait_ge(S["x_pn"], h + 1)
                for q in range(4):
                    for i in range(4 * q, 4 * q + 4):
                        m, c = divmod(i, NC)
                        mm = pe.transpose(ps[:, 4 + q, (i % 4) * P:(i % 4 + 1) * P],
                                          flat(dd)[:, c * N_MEM + m * P:c * N_MEM + (m + 1) * P], ident[:, :])
                    mm.then_inc(S["x_pt"], 1)
                if nxt is not None:
                    project(nxt, st, cum["out"])
                pe.wait_ge(S["x_ptc"], 4 * h + 4)
                for half in range(2):
                    for m in range(2):
                        mm = pe.matmul(ps[:, 2 + half, :], vm[:, m, :],
                                       flat(pair)[:, m * SEQ + half * HALF:m * SEQ + (half + 1) * HALF],
                                       start=(m == 0), stop=(m == 1))
                    mm.then_inc(S["x_o"], 1)
                if nxt is not None:
                    project(nxt, st, cum["end"])

            with pe.Fori(0, GH - 1) as h:
                gdn(h, (GDN, h + 1))
            gdn(GH - 1, (MLSTM, 0))
            with pe.Fori(0, MH - 1) as h:
                mlstm(h, (MLSTM, h + 1))
            mlstm(MH - 1, (MEM, 0))
            with pe.Fori(0, XH - 1) as h:
                memory(h, (MEM, h + 1))
            memory(XH - 1, None)

            for t in range(NC):
                pe.wait_ge(S["o_mlo"], t + 1)
                if t >= 2:
                    pe.wait_ge(S["o_y"], 2 * (t - 1))
                for i in range(KT):
                    for j in range(2):
                        if t == 0:
                            pe.wait_ge(S[f"o_lo{j}"], i + 1)
                        kt = j * KT + i
                        for half in range(2):
                            for term in range(TERMS):
                                lhs = (mx_hi, mx_hi, mx_lo)[term][t % 2]
                                w = (wo_hi, wo_lo, wo_hi)[term][j]
                                mm = pe.matmul(ps[:, 2 + 2 * (t % 2) + half, :], lhs[:, kt, :],
                                               w[:, i, half * HALF:(half + 1) * HALF],
                                               start=(i == 0 and j == 0 and term == 0),
                                               stop=(i == KT - 1 and j == 1 and term == TERMS - 1))
                            if i == KT - 1 and j == 1:
                                mm.then_inc(S["o_ps"], 1)


_INS = ["x", "mem", "norm_g", "w_in", "conv_w", "gdn_a_log", "gdn_dt_bias", "gdn_norm_g", "mlstm_i_bias",
        "mlstm_f_bias", "mlstm_norm_g", "mem_norm_g", "w_mem_kv", "w_out", "final_norm_g"]


def kernel(**inputs):
    import concourse.bacc as bacc
    from concourse.bass_utils import run_bass_kernel_spmd as run

    nc = bacc.Bacc("TRN2", target_bir_lowering=False, num_devices=1)
    arrays, args = {}, []
    for name in _INS:
        a = np.ascontiguousarray(inputs[name])
        arrays[f"in_{name}"] = a
        ap = nc.dram_tensor(f"in_{name}", a.shape, F32, kind="ExternalInput").ap()
        args.append(ap if name == "final_norm_g" else ap[0])
    out = nc.dram_tensor("out_0", (1, SEQ, D_MODEL), F32, kind="ExternalOutput").ap()[0]
    mixed = nc.dram_tensor("mixed", (MIX, SEQ), F32, kind="Internal").ap()
    build(nc, *args, out, mixed)
    r = run(nc, [arrays], core_ids=[0])
    return r.results[0]["out_0"]
```

```python
from contextlib import ExitStack

import concourse.bass as bass
import numpy as np
from concourse import mybir

F32 = mybir.dt.float32
F32R = mybir.dt.float32r
ALU = mybir.AluOpType
ACT = mybir.ActivationFunctionType
AX = mybir.AxisListType

P = 128
D_MODEL = 1024
SEQ = 1024
N_MEM = 256
MIX = 2 * D_MODEL
KT = D_MODEL // P
NC = SEQ // P
HALF = 512
GH, MH, XH = 6, 6, 4
HEADS = GH + MH + XH
GW, MW, XW = GH * P, MH * P, XH * P
EPS = 1e-6
SCALE = float(P) ** -0.5
WIDTHS = [GW, GW, GW, GH, GH, GW, MW, MW, MW, MH, MH, MW, MW, XW, XW]
(G_Q, G_K, G_V, G_A, G_B, G_Z, M_Q, M_K, M_V, M_I, M_F, M_O, M_Z, X_Q, X_Z, IN_COLS) = \
    [int(v) for v in np.cumsum([0] + WIDTHS)]
GDN, MLSTM, MEM = range(3)
BLOCKS = {GDN: [G_Q, G_K, G_V, G_Z], MLSTM: [M_Q, M_K, M_V, M_O, M_Z], MEM: [X_Q, X_Z]}
SLOTS = {GDN: [0, 1, 0, 1], MLSTM: [0, 1, 2, 0, 1], MEM: [0, 1]}
TERMS = 3
UNIT = KT * TERMS
LEVELS = 7
R_GA, R_MF, R_GB, R_MI = 0, 32, 64, 96
T_G, T_E, T_F, T_L, T_X, T_NE, NTAB = 0, 1, 2, 3, 4, 5, 6
PAST = 3


def uses(slot, head, block):
    kind, h = head
    n = SLOTS[kind][:block + 1].count(slot)
    if slot == 2:
        return 1 + h + n
    return {GDN: 2 * h, MLSTM: 2 * GH + 2 * h, MEM: 2 * GH + 2 * MH + h}[kind] + n + KV_USES


KV_USES = 4
UNITS = {GDN: 8, MLSTM: 10, MEM: 4}


def units_before(head):
    kind, h = head
    return PRE_UNITS + {GDN: 8 * h, MLSTM: 8 * GH + 10 * h, MEM: 8 * GH + 10 * MH + 4 * h}[kind]


PRE_UNITS = 2 * XH + 2
ALL_UNITS = PRE_UNITS + 8 * GH + 10 * MH + 4 * XH

FILL = {
    GDN: [("decay", 27), ("queries", 12), ("keys", 12), ("pairs", 16), ("a0", 2), ("a1", 8)]
         + [(f"b{l}", 4) for l in range(1, LEVELS)]
         + [(f"t{l}", 4) for l in range(1, LEVELS - 1)]
         + [(f"{s}{c}", n) for c in range(NC) for s, n in (("r", 3), ("y", 2), ("s", 3))] + [("turn", 8)],
    MLSTM: [("v", 16), ("decay", 16), ("pairs", 24), ("k", 16), ("o", 16)]
           + [(f"c{c}", 8) for c in range(NC)] + [("turn", 24)],
    MEM: [("v", 8), ("scores", 8), ("probs", 40), ("out", 24)],
    (MLSTM, MEM): [("v", 8), ("decay", 8), ("pairs", 4), ("k", 4), ("o", 4)] + [(f"c{c}", 5) for c in range(NC)]
                  + [("turn", 24)],
}


def order(kind):
    if kind == GDN:
        s = ["decay", "queries", "keys", "pairs", "a0"]
        for l in range(1, LEVELS):
            s += [f"b{l}"] + [f"t{l}"] * (l < LEVELS - 1) if l > 1 else ["a1", "b1", "t1"]
        for c in range(NC):
            s += [f"r{c}", f"y{c}", f"s{c}"]
        return s + ["turn"]
    if kind == MLSTM:
        return ["v", "decay", "pairs", "k", "o"] + [f"c{c}" for c in range(NC)] + ["turn"]
    return ["v", "scores", "probs", "out"]


def plan(kind, nxt):
    total = UNITS[nxt] * UNIT if nxt is not None else 0
    fill, done, out = dict(FILL.get((kind, nxt), FILL[kind])), 0, {}
    for s in order(kind):
        done = min(total, done + fill[s])
        out[s] = done
    out["end"] = total
    return out


class Steps:

    def __init__(self, eng, sem, base=0):
        self.eng, self.sem, self.base, self.n = eng, sem, base, 0

    def done(self, ins):
        self.n += 1
        ins.then_inc(self.sem, 1)
        self.eng.wait_ge(self.sem, self.base + self.n)


def build(nc, x, mem, norm_g, w_in, conv_w, a_log, dt_bias, gdn_g, i_bias, f_bias, mlstm_g,
          mem_g, w_kv, w_out, final_g, out, mixed):
    ctx = ExitStack()
    with ctx:
        place = [16640]

        def sb(name, shape, dt=F32, offset=None):
            size = (4 * int(np.prod(shape[1:])) + 31) // 32 * 32
            if offset is None:
                offset = place[0]
                place[0] += size
            return nc.alloc_sbuf_tensor_at(name, shape, dt, offset=offset)

        def sem(name):
            return ctx.enter_context(nc.semaphore(name))

        def flat(t):
            return t[:, :, :, :].rearrange("p a b c -> p (a b c)")

        def over(ap, n):
            return ap.unsqueeze(2).broadcast_to([P, ap.shape[1], n])

        def each(ap, n):
            return ap.unsqueeze(1).broadcast_to([P, n, ap.shape[1]])

        ident = sb("ident", [P, P])
        upper = sb("upper", [P, P])
        later = sb("later", [P, P])
        later_r = sb("later_r", [P, P], F32R)
        ones = sb("ones", [P, P])
        first_t = sb("first_t", [P, P])
        level_mask = sb("level_mask", [P, LEVELS, 64])
        minus_half = sb("minus_half", [P, 16])
        params = sb("params", [P, 80])
        gcol = sb("gcol", [P, 4])
        tab = sb("tab", [P, GH + MH, NTAB, NC])
        guard = sb("guard", [P, MH, NC])
        ht = sb("ht", [P, NTAB, NC])
        g_hi = sb("g_hi", [P, NC], F32R)
        g_lo = sb("g_lo", [P, NC])
        hguard = sb("hguard", [P, NC])
        hconv = sb("hconv", [P, 12])
        hnorm = sb("hnorm", [P, 1])
        ss_tiles = sb("ss_tiles", [P, 16])
        rstd_tiles = sb("rstd_tiles", [P, 16])
        sm = sb("sm", [P, 12, 16])
        state = sb("state", [P, P + 1])
        rhs = sb("rhs", [P, 2, P])
        zed = sb("zed", [P, 2, P])
        param_rows = sb("param_rows", [80, P], offset=place[0])
        carried = sb("carried", [P, 2, P + 1])
        kv_at = place[0]
        kv = sb("kv", [P, 2 * XH, N_MEM])
        hkv = sb("hkv", [P, 2, N_MEM])
        vm = sb("vm", [P, 2, P])
        xn_hi = sb("xn_hi", [P, KT, SEQ], F32R)
        xn_lo_at = place[0]
        xn_lo = sb("xn_lo", [P, KT, SEQ], F32R)
        late_at = place[0]
        w_raw = [sb(f"w_raw{s}", [P, KT, P]) for s in range(3)]
        w_hi = [sb(f"w_hi{s}", [P, KT, P], F32R) for s in range(3)]
        w_lo = [sb(f"w_lo{s}", [P, KT, P], F32R) for s in range(3)]
        raw_at = place[0]
        raw = sb("raw", [P, 5, PAST + SEQ])
        work_at = place[0]
        vt = sb("vt", [P, SEQ])
        sz_at = place[0]
        sz = sb("sz", [P, SEQ])
        dd_at = place[0]
        dd = sb("dd", [P, NC, 2, P])
        pair_at = place[0]
        pair = sb("pair", [P, NC, 2, P])
        mix_at = place[0]
        mix = sb("mix", [P, SEQ])
        spare_at = place[0]
        qk = sb("qk", [P, NC, 2, P])
        gu_at = place[0]
        gu = sb("gu", [P, NC, P])
        minv_at = place[0]
        minv = sb("minv", [P, NC, P])
        minv_t = sb("minv_t", [P, NC, P])
        xx_at = place[0]
        xx = [sb(f"xx{i}", [P, NC, P]) for i in range(2)]
        fk_at = place[0]
        fk = sb("fk", [P, NC, P])
        nv = sb("nv", [P, NC, P])
        work_end = place[0]
        assert work_end <= 229368, work_end
        gu_hi = sb("gu_hi", [P, NC, P], F32R, offset=gu_at)
        gu_lo = sb("gu_lo", [P, NC, P], F32R, offset=fk_at)
        v_ext = sb("v_ext", [P, NC, P + 1], offset=minv_at)
        num_den = sb("num_den", [P, NC, P + 1], offset=xx_at)
        spot = [work_at]

        def early(name, shape, dt=F32):
            t = sb(name, shape, dt, offset=spot[0])
            spot[0] += (4 * int(np.prod(shape[1:])) + 31) // 32 * 32
            assert spot[0] <= work_end, name
            return t

        mem_hi = early("mem_hi", [P, KT, N_MEM], F32R)
        mem_lo = early("mem_lo", [P, KT, N_MEM], F32R)
        g_rows = early("g_rows", [P, 2, D_MODEL])
        x_in = early("x_in", [P, 3, D_MODEL])
        x_tok = early("x_tok", [P, 2, D_MODEL])
        rows = early("rows", [P, SEQ])
        z_row = early("z_row", [P, SEQ])
        m_row = early("m_row", [P, SEQ + 8])
        i_row, u_row = x_in[:, 0, :], x_in[:, 1, :]
        e_row, l_row = x_tok[:, 0, :], x_tok[:, 1, :]
        TILE = 4 * D_MODEL
        raw2_at = (raw_at + 8 * (PAST + SEQ) + 31) // 32 * 32

        def tile(name, at, dt=F32R):
            return sb(name, [P, KT, P], dt, offset=at)

        wo_lo = [sb("wo_lo", [P, KT, D_MODEL], F32R, offset=spare_at), xn_lo]
        wo_raw = [sb(f"wo_raw{i}", [P, KT, D_MODEL], offset=at) for i, at in enumerate((spare_at, xn_lo_at))]
        wo_hi = [[sb(f"wo_hi{k}", [P, D_MODEL], F32R, offset=late_at + i * TILE)
                  for k, i in enumerate((2, 5, 8, 0, 1, 3, 4, 6))], [xn_hi[:, k, :] for k in range(KT)]]
        mx_hi = [tile(f"mx_hi{i}", at) for i, at in enumerate((spare_at + 8 * TILE, dd_at, pair_at, raw_at))]
        mx_lo = [tile(f"mx_lo{i}", at) for i, at in enumerate((raw2_at, dd_at + TILE, pair_at + TILE, raw_at + TILE))]
        mx_raw = [tile("mx_raw0", raw2_at + 2 * TILE, F32), vt[:, :].rearrange("p (k t) -> p k t", k=KT)]
        x_t = [sb("x_t0", [P, D_MODEL], offset=raw2_at + TILE), sb("x_t1", [P, D_MODEL], offset=late_at + 7 * TILE)]
        y = [sb("y0", [P, D_MODEL], offset=sz_at), sb("y1", [P, D_MODEL], offset=mix_at)]
        fg_row = sb("fg_row", [P, D_MODEL], offset=kv_at)
        y_sq = sb("y_sq", [P, D_MODEL], offset=kv_at + 4 * D_MODEL)

        ps = nc.alloc_psum_tensor("ps", [P, 8, HALF], F32)

        names = """consts tiny gw_zero x_loaded0 x_loaded1 x_loaded2 x_square x_rstd x_scaled x_turned x_hi
            x_lo rowz_loaded grows0 grows1 gate_act gate_rows gate_turned gate_tab gate_sum gate_exp gate_m
            pool_early pool_turn params_turned params_out unit_done unit_out head_done mix_stored
            g_tab g_tap g_conv g_silu g_sq g_gu g_sse g_rk g_w g_decay g_exp g_dm g_dd g_kq g_pair g_qt g_kt g_fk
            g_vt g_nv g_mt0 g_m0 g_a g_x g_b g_m g_c g_mt g_xz g_ks g_qs g_r g_y g_z g_up g_att g_s
            g_cq g_o g_osq g_oms g_ors g_og g_ot g_dve
            m_tab m_qk m_sig m_gate m_gu m_v m_ve m_decay m_exp m_dd m_pair m_pm m_k m_fk m_o m_sg
            m_up m_s m_qc m_cq m_pv m_nd m_h m_hsq m_ms m_rs m_og m_ot m_dve
            x_kv x_q x_silu x_v x_vm x_sc x_nb x_p x_pn x_pt x_ptc x_o x_dve
            o_load o_load0 o_load1 o_load2 o_load3 o_hi o_lo o_fg o_mx0 o_mx1 o_mhi o_mlo o_x0 o_x1
            o_used o_y o_sq o_ms o_rs o_out o_st0 o_st1 early_dve early_pool early_act""".split()
        S = {n: sem(n) for n in names}
        w_loaded = [sem(f"w_loaded{s}") for s in range(3)]
        w_hi_done = [sem(f"w_hi_done{s}") for s in range(3)]
        w_split = [sem(f"w_split{s}") for s in range(3)]

        w_cols = w_in.rearrange("(k p) n -> p k n", p=P)
        kv_cols = w_kv.rearrange("(k p) n -> p k n", p=P)
        wo_rows = w_out.rearrange("(k p) n -> p k n", p=P)
        mixed_cols = mixed.rearrange("(k p) t -> p k t", p=P)

        def mixed_load(sp, pair, i):
            half = i // 2
            sp.dma_start(mx_raw[i % 2][:, :, :], mixed_cols[:, half * KT:(half + 1) * KT,
                                                           bass.ds(pair * 2 * P + i % 2 * P, P)])\
                .then_inc(S[f"o_mx{i % 2}"], 16)

        TILES = [(mem, 0), (mem, 1)] + [(x, t) for t in range(NC)]

        def halves(t, l):
            v = t[:, :, :].rearrange("p c (n two b) -> p c n two b", two=2, b=1 << l)
            return v[:, :, :, 0, :], v[:, :, :, 1, :]

        def halves_of(t, c, l):
            v = t[:, c, :].rearrange("p (n two b) -> p n two b", two=2, b=1 << l)
            return v[:, :, 0, :], v[:, :, 1, :]

        def x_of(l):
            return xx[0] if l == LEVELS - 1 else xx[1]

        def packed(bank, l):
            return ps[:, bank, :].rearrange("p (c n b) -> p c n b", c=NC, b=1 << l)

        block = ctx.enter_context(nc.Block())

        @block.sync
        def _(sp):
            def load(slot, n, src):
                if n is not None:
                    sp.wait_ge(w_split[slot], n)
                sp.dma_start(w_raw[slot][:, :, :], src).then_inc(w_loaded[slot], 16)

            def head_blocks(kind, h):
                for b, (first, slot) in enumerate(zip(BLOCKS[kind], SLOTS[kind])):
                    load(slot, uses(slot, (kind, h), b) - 1,
                         w_cols[:, :, bass.ds(h * P + first, P)])

            def x_tile(i):
                src, t = TILES[i]
                if i >= 3:
                    sp.wait_ge(S["x_scaled"], i - 2)
                sp.dma_start(x_in[:, i % 3, :], src[t * P:(t + 1) * P, :]).then_inc(S[f"x_loaded{i % 3}"], 16)

            x_tile(0)
            for r, g in ((1, mem_g), (0, norm_g)):
                sp.dma_start(g_rows[:, r, :], g.partition_broadcast(P)).then_inc(S[f"grows{r}"], 16)
            x_tile(1)
            load(0, None, kv_cols[:, :, 0:P])
            x_tile(2)
            load(1, None, kv_cols[:, :, P:2 * P])
            sp.wait_ge(S["gw_zero"], 1)
            for first, row in ((G_A, R_GA), (M_F, R_MF), (G_B, R_GB), (M_I, R_MI)):
                sp.dma_start(w_raw[2][:, :, row:row + GH], w_cols[:, :, first:first + GH])\
                    .then_inc(w_loaded[2], 16)
            for src, row, col in ((dt_bias, R_GA, 1), (f_bias, R_MF, 1), (a_log, R_GA, 2), (i_bias, R_MF, 3)):
                sp.dma_start(gcol[row:row + GH, col:col + 1], src.rearrange("(h a) -> h a", a=1))\
                    .then_inc(S["tiny"], 16)
            taps = conv_w.shape[0] * conv_w.shape[1] // P
            for r in range(conv_w.shape[0]):
                n = conv_w.shape[1] // P
                sp.dma_start(param_rows[r * n:(r + 1) * n, :], conv_w[r].rearrange("(b p) -> b p", p=P))\
                    .then_inc(S["rowz_loaded"], 16)
            sp.dma_start(param_rows[taps:taps + 1, :], gdn_g.rearrange("(a p) -> a p", a=1))\
                .then_inc(S["rowz_loaded"], 16)
            sp.dma_start(param_rows[taps + 1:taps + 1 + MH, :], mlstm_g).then_inc(S["rowz_loaded"], 16)
            for i in range(3, 2 + NC):
                x_tile(i)
                if 4 <= i:
                    b = i - 2
                    load(b % 2, b // 2, kv_cols[:, :, b * P:(b + 1) * P])
            head_blocks(GDN, 0)
            with sp.Fori(1, GH) as h:
                head_blocks(GDN, h)
            with sp.Fori(0, MH) as h:
                head_blocks(MLSTM, h)
            with sp.Fori(0, XH) as h:
                head_blocks(MEM, h)

            sp.wait_ge(S["head_done"], GH + MH + 1)
            for q in range(2):
                sp.dma_start(wo_raw[0][:, 4 * q:4 * q + 4, :], wo_rows[:, 4 * q:4 * q + 4, :])\
                    .then_inc(S["o_load"], 16)
            sp.dma_start(x_t[0][:, :], x[0:P, :]).then_inc(S["o_x0"], 16)
            sp.wait_ge(S["mix_stored"], 16 * 9)
            mixed_load(sp, 0, 0)
            sp.wait_ge(S["unit_done"], ALL_UNITS)
            for g in range(4):
                sp.dma_start(wo_raw[1][:, 2 * g:2 * g + 2, :], wo_rows[:, KT + 2 * g:KT + 2 * g + 2, :])\
                    .then_inc(S[f"o_load{g}"], 16)
            sp.dma_start(x_t[1][:, :], x[P:2 * P, :]).then_inc(S["o_x1"], 16)
            sp.wait_ge(S["x_sc"], 4 * XH)
            mixed_load(sp, 0, 1)
            sp.wait_ge(S["head_done"], HEADS + 1)
            sp.dma_start(fg_row[:, :], final_g.partition_broadcast(P)).then_inc(S["o_fg"], 16)
            sp.wait_ge(S["mix_stored"], 16 * (HEADS + 1))
            for n in (2, 3):
                sp.wait_ge(S["o_mlo"], n - 1)
                mixed_load(sp, 0, n)

            def out_pair(pair, ahead):
                def load(i):
                    if ahead:
                        sp.wait_ge(S["o_mlo"], 4 * pair + 3 + i)
                        mixed_load(sp, pair + 1, i)

                load(0)
                load(1)
                for r in range(2):
                    sp.wait_ge(S["o_out"], 2 * pair + r + 1)
                    sp.dma_start(out[bass.ds(pair * 2 * P + r * P, P), :], y[r][:, :]).then_inc(S[f"o_st{r}"], 16)
                    if ahead:
                        sp.dma_start(x_t[r][:, :], x[bass.ds(pair * 2 * P + (2 + r) * P, P), :]).then_inc(S[f"o_x{r}"], 16)
                    load(2 + r)

            with sp.Fori(0, NC // 2 - 1) as pair_n:
                out_pair(pair_n, True)
            out_pair(NC // 2 - 1, False)
            for r in range(2):
                sp.wait_ge(S[f"o_st{r}"], 16 * (NC // 2))

        @block.gpsimd
        def _(pool):
            def plain():
                pool.sem_inc(S["pool_turn"], 1)

            early = Steps(pool, S["early_pool"])
            pool.memset(gcol[:, :], 0.0)
            pool.memset(w_raw[2][:, :, :], 0.0).then_inc(S["gw_zero"], 1)
            pool.memset(minus_half[:, :], -0.5)
            early.done(pool.memset(ones[:, :], 1.0))
            pool.affine_select(out=upper[:, :], in_=ones[:, :], compare_op=ALU.is_ge, fill=0.0, base=0,
                               pattern=[[1, P]], channel_multiplier=-1)
            early.done(pool.affine_select(out=later[:, :], in_=ones[:, :], compare_op=ALU.is_gt, fill=0.0, base=0,
                                          pattern=[[-1, P]], channel_multiplier=1))
            pool.affine_select(out=ident[:, :], in_=upper[:, :], compare_op=ALU.is_ge, fill=0.0, base=0,
                               pattern=[[-1, P]], channel_multiplier=1).then_inc(S["consts"], 1)
            pool.tensor_copy(later_r[:, :], later[:, :])
            pool.memset(rows[:, :], 0.0)
            pool.memset(m_row[:, :], 0.0)
            pool.memset(raw[:, 0:3, 0:PAST], 0.0)

            for i in range(2 + NC):
                pool.wait_ge(S["x_square"], i + 1)
                early.done(pool.tensor_scalar(ss_tiles[:, i:i + 1], ss_tiles[:, i:i + 1], 1.0 / D_MODEL, EPS,
                                              ALU.mult, ALU.add))
                pool.tensor_tensor(rstd_tiles[:, i:i + 1], ss_tiles[:, i:i + 1], minus_half[:, 0:1], ALU.pow)\
                    .then_inc(S["x_rstd"], 1)
            pool.memset(level_mask[:, :, :], -1.0)
            early.done(pool.memset(first_t[:, :], -1.0))
            ft = first_t[:, :].rearrange("p (n r) -> p n r", r=2)
            early.done(pool.affine_select(out=ft, in_=ft, compare_op=ALU.is_equal, fill=0.0, base=0,
                                          pattern=[[-2, P // 2], [0, 2]], channel_multiplier=1))
            early.done(pool.affine_select(out=ft, in_=ft, compare_op=ALU.is_gt, fill=0.0, base=0,
                                          pattern=[[0, P // 2], [1, 2]], channel_multiplier=0))
            for l in range(LEVELS):
                b = 1 << l
                m = level_mask[:, l, :].rearrange("p (n r) -> p n r", r=b)
                early.done(pool.affine_select(out=m, in_=m, compare_op=ALU.is_ge, fill=0.0, base=-b,
                                              pattern=[[-2 * b, 64 // b], [0, b]], channel_multiplier=1))
                early.done(pool.affine_select(out=m, in_=m, compare_op=ALU.is_ge, fill=0.0, base=2 * b - 1,
                                              pattern=[[2 * b, 64 // b], [0, b]], channel_multiplier=-1))

            def split_hi_slot2(nxt):
                if nxt[0] == MLSTM:
                    n = uses(2, nxt, 2)
                    pool.wait_ge(w_loaded[2], 48 + n * 16)
                    pool.wait_ge(S["unit_done"], units_before(nxt) - 4)
                    plain()
                    pool.tensor_copy(w_hi[2][:, :, :], w_raw[2][:, :, :]).then_inc(w_hi_done[2], 1)

            def gdn(h, nxt):
                pool.wait_ge(S["g_tab"], h + 1)
                pool.tensor_tensor(gu_hi[:, :, :], each(upper[:, :], NC), over(g_hi[:, :].bitcast(F32), P), ALU.mult)
                pool.tensor_tensor(gu_lo[:, :, :], each(upper[:, :], NC), over(g_lo[:, :], P), ALU.mult)\
                    .then_inc(S["g_gu"], 1)
                split_hi_slot2(nxt)
                pool.memset(xx[0][:, :, :], 0.0).then_inc(S["g_xz"], 1)
                pool.tensor_copy(minv[:, :, :], each(ident[:, :], NC)).then_inc(S["g_m0"], 1)
                pool.wait_ge(S["g_exp"], 2 * h + 2)
                pool.tensor_tensor(dd[:, :, 1, :], xx[1][:, :, :], each(upper[:, :], NC), ALU.mult).then_inc(S["g_dm"], 1)
                pool.wait_ge(S["g_sse"], h + 1)
                pool.tensor_tensor(sm[:, 1, :], sm[:, 0, :], minus_half[:, :], ALU.pow).then_inc(S["g_rk"], 1)
                pool.wait_ge(S["g_pair"], 4 * h + 4)
                pool.tensor_tensor(minv_t[:, :, :], pair[:, :, 0, :], each(first_t[:, :], NC), ALU.mult)\
                    .then_inc(S["pool_early"], 1)
                pool.wait_ge(S["pool_early"], h + 1)
                pool.tensor_tensor(minv_t[:, :, :], minv_t[:, :, :], each(ident[:, :], NC), ALU.add)\
                    .then_inc(S["g_mt0"], 1)
                for half in range(2):
                    c4 = slice(4 * half, 4 * half + 4)
                    pool.wait_ge(S["g_oms"], 2 * h + half + 1)
                    pool.tensor_tensor(sm[:, 6, c4], sm[:, 5, c4], minus_half[:, c4], ALU.pow).then_inc(S["g_ors"], 1)

            def mlstm(h, nxt):
                pool.wait_ge(S["m_tab"], h + 1)
                pool.tensor_tensor(gu_hi[:, :, :], each(upper[:, :], NC), over(g_hi[:, :].bitcast(F32), P), ALU.mult)
                pool.tensor_tensor(gu_lo[:, :, :], each(upper[:, :], NC), over(g_lo[:, :], P), ALU.mult)\
                    .then_inc(S["m_gu"], 1)
                split_hi_slot2(nxt)
                pool.wait_ge(S["m_sig"], 2 * h + 2)
                pool.tensor_tensor(sz[:, :], sz[:, :], raw[:, 4, PAST:], ALU.mult).then_inc(S["m_gate"], 1)
                pool.wait_ge(S["m_exp"], 2 * h + 2)
                pool.tensor_tensor(dd[:, 0:4, :, :].rearrange("p a b t -> p (a b) t"),
                                   dd[:, 4:8, :, :].rearrange("p a b t -> p (a b) t"),
                                   each(upper[:, :], NC), ALU.mult).then_inc(S["m_dd"], 1)
                for half in range(2):
                    c4 = slice(4 * half, 4 * half + 4)
                    pool.wait_ge(S["m_ms"], 2 * h + half + 1)
                    pool.tensor_tensor(sm[:, 6, c4], sm[:, 5, c4], minus_half[:, c4], ALU.pow).then_inc(S["m_rs"], 1)

            def memory(h):
                pool.wait_ge(S["head_done"], h + GH + MH + 1)
                plain()
                pool.tensor_copy(hkv[:, 0, :], kv[:, bass.ds(h, 1), :].rearrange("p a m -> p (a m)"))
                pool.tensor_copy(hkv[:, 1, :], kv[:, bass.ds(h + XH, 1), :].rearrange("p a m -> p (a m)"))\
                    .then_inc(S["x_kv"], 1)
                pool.wait_ge(S["unit_out"], units_before((MEM, h)) + 2)
                plain()
                pool.tensor_copy(vt[:, :], raw[:, 0, PAST:]).then_inc(S["x_q"], 1)

            with pool.Fori(0, GH - 1) as h:
                gdn(h, (GDN, h + 1))
            gdn(GH - 1, (MLSTM, 0))
            with pool.Fori(0, MH - 1) as h:
                mlstm(h, (MLSTM, h + 1))
            mlstm(MH - 1, (MEM, 0))
            with pool.Fori(0, XH) as h:
                memory(h)

            with pool.Fori(0, NC) as t:
                pool.wait_ge(S["o_ms"], t + 1)
                pool.tensor_tensor(sm[:, 1, 0:1], sm[:, 0, 0:1], minus_half[:, 0:1], ALU.pow).then_inc(S["o_rs"], 1)

        @block.scalar
        def _(act):
            def unit_copy(head, u, free):
                act.wait_ge(S["unit_done"], units_before(head) + u + 1)
                b, half = u // 2, u % 2
                if half == 0:
                    free(b)
                act.activation(raw[:, b, PAST + half * HALF:PAST + (half + 1) * HALF], ps[:, half, :], ACT.Copy)\
                    .then_inc(S["unit_out"], 1)

            def advance(nxt, st, upto, free, more=True):
                while (st[0] + 1) * UNIT <= upto:
                    u = st[0]
                    st[0] += 1
                    unit_copy(nxt, u, free)
                    slot = SLOTS[nxt[0]][u // 2]
                    if u % 2 and slot < 2 and more:
                        n = uses(slot, nxt, u // 2) + 1
                        act.wait_ge(w_loaded[slot], 16 * n)
                        act.activation(w_hi[slot][:, :, :], w_raw[slot][:, :, :], ACT.Copy).then_inc(w_hi_done[slot], 1)

            def split_hi(slot, n, loaded, free):
                act.wait_ge(w_loaded[slot], loaded)
                if free is not None:
                    act.wait_ge(S["unit_done"], free)
                act.activation(w_hi[slot][:, :, :], w_raw[slot][:, :, :], ACT.Copy).then_inc(w_hi_done[slot], 1)

            early = Steps(act, S["early_act"])

            def square(i):
                act.wait_ge(S[f"x_loaded{i % 3}"], 16 * (i // 3 + 1))
                if i:
                    act.wait_ge(S["x_square"], i)
                act.activation(nv[:, :, :].rearrange("p c t -> p (c t)"), x_in[:, i % 3, :], ACT.Square,
                               accum_out=ss_tiles[:, i:i + 1]).then_inc(S["x_square"], 1)

            square(0)
            for i in range(2 + NC + 1):
                if i + 1 < 2 + NC:
                    square(i + 1)
                if i >= 1:
                    j = i - 1
                    hi = (mem_hi[:, :, j * P:(j + 1) * P] if j < 2 else xn_hi[:, :, (j - 2) * P:(j - 1) * P])
                    for q in range(2):
                        act.wait_ge(S["x_turned"], 2 * j + q + 1)
                        act.activation(hi[:, 4 * q:4 * q + 4, :],
                                       ps[:, 4 + 2 * (j % 2) + q, :].rearrange("p (k t) -> p k t", k=4), ACT.Copy)\
                            .then_inc(S["x_hi"], 1)
                if 1 <= i <= 2 * XH:
                    b = i - 1
                    split_hi(b % 2, b // 2 + 1, 16 * (b // 2 + 1), b - 1 if b >= 2 else None)
                if i == 2 * XH + 1:
                    split_hi(2, 1, 64, None)
                if 3 <= i:
                    b = i - 3
                    act.wait_ge(S["unit_done"], b + 1)
                    act.activation(kv[:, b, :], ps[:, b % 2, 0:N_MEM], ACT.Copy).then_inc(S["unit_out"], 1)
            for slot in range(2):
                split_hi(slot, KV_USES + 1, 16 * (KV_USES + 1), 2 * XH - 1 + slot)
            act.sem_inc(S["mix_stored"], 16)
            act.preload_act_table_set("natural_log_exp_and_others")
            act.wait_ge(S["tiny"], 64)
            act.activation(gcol[R_GA:R_GA + GH, 2:3], gcol[R_GA:R_GA + GH, 2:3], ACT.Exp).then_inc(S["gate_exp"], 1)
            act.wait_ge(S["gate_m"], 1)
            for half in range(2):
                cols = slice(half * HALF, (half + 1) * HALF)
                act.wait_ge(S["unit_done"], 2 * XH + half + 1)
                act.activation(z_row[0:64, cols], ps[0:64, half, :], ACT.Identity, bias=gcol[0:64, 1:2],
                               scale=gcol[0:64, 0:1])
                act.activation(rows[64:96, cols], ps[64:96, half, :], ACT.Exp, scale=-1.0)
                act.activation(i_row[32:64, cols], ps[96:128, half, :], ACT.Copy).then_inc(S["unit_out"], 1)
            act.wait_ge(S["unit_out"], 2 * XH + 2)
            early.done(act.activation(e_row[0:64, :], z_row[0:64, :], ACT.Abs))
            act.activation(e_row[0:64, :], e_row[0:64, :], ACT.Exp, scale=-1.0).then_inc(S["gate_act"], 1)
            act.wait_ge(S["gate_rows"], 1)
            act.activation(l_row[0:64, :], u_row[0:64, :], ACT.Ln).then_inc(S["gate_act"], 1)
            st = [0]
            advance((GDN, 0), st, UNITS[GDN] * UNIT, lambda b: None)
            act.wait_ge(S["gate_tab"], 1)
            act.wait_ge(S["gate_turned"], 3)
            act.activation(tab[:, GH:, T_X, :].rearrange("p h c -> p c h"),
                           ps[:, 4:6, :].rearrange("p a (c r) -> p (a c) r", c=4)[:, :, R_MI:R_MI + MH], ACT.Exp)
            act.activation(guard[:, :, :].rearrange("p h c -> p c h"),
                           ps[:, 6, 0:NC * 32].rearrange("p (c r) -> p c r", c=NC)[:, :, 0:MH], ACT.Exp, scale=-1.0)\
                .then_inc(S["gate_exp"], 1)
            act.wait_ge(S["gate_sum"], 1)
            act.activation(tab[:, :, T_E:T_L + 1, :].rearrange("p h k c -> p k h c"),
                           ps[:, 7, 0:3 * 96].rearrange("p (k h c) -> p k h c", k=3, h=GH + MH), ACT.Exp)\
                .then_inc(S["gate_exp"], 1)

            dd_spare = flat(dd)[:, SEQ:].rearrange("p (c t) -> p c t", c=NC)

            def squares(ready, base, src, spare, c, out):
                act.wait_ge(ready, base + c + 1)
                act.activation(spare[:, c, :], src[:, c, :], ACT.Square, accum_out=sm[:, 8, c:c + 1]).then_inc(out, 1)

            def gdn(h, nxt):
                cum, st = plan(GDN, nxt and nxt[0]), [0]

                def free(b):
                    if b < 3:
                        act.wait_ge(S["g_conv"], 3 * h + b + 1)

                act.wait_ge(S["g_tab"], h + 1)
                for b, dst in ((1, flat(pair)[:, SEQ:]), (2, nv[:, :, :].rearrange("p c t -> p (c t)"))):
                    act.wait_ge(S["unit_out"], units_before((GDN, h)) + 2 * b + 2)
                    act.activation(dst, raw[:, b, 0:SEQ], ACT.Copy, scale=hconv[:, b:b + 1]).then_inc(S["g_tap"], 1)
                for half in range(2):
                    act.wait_ge(S["g_decay"], 2 * h + half + 1)
                    act.activation(xx[1][:, 4 * half:4 * half + 4, :],
                                   ps[:, 6 + half, :].rearrange("p (c t) -> p c t", c=4), ACT.Exp)\
                        .then_inc(S["g_exp"], 1)
                for b, (src, dst) in enumerate(((flat(pair)[:, 0:SEQ], qk[:, :, 1, :]), (flat(pair)[:, SEQ:], qk[:, :, 0, :]))):
                    act.wait_ge(S["g_conv"], 3 * h + b + 1)
                    act.activation(dst, src.rearrange("p (c t) -> p c t", c=NC), ACT.Silu).then_inc(S["g_silu"], 1)
                    if b == 0:
                        advance(nxt, st, min(2 * UNIT, cum["queries"]), free)
                    for c in range(NC):
                        act.wait_ge(S["g_kt" if b else "g_qt"], 2 * h + c // 4 + 1)
                        act.activation(minv_t[:, c, :] if b else dd[:, c, 0, :],
                                       ps[:, 2 + 2 * b + c // 4, (c % 4) * P:(c % 4 + 1) * P],
                                       ACT.Square, accum_out=sm[:, 0, 2 * c + 1 - b:2 * c + 2 - b]).then_inc(S["g_sq"], 1)
                act.wait_ge(S["g_conv"], 3 * h + 3)
                act.activation(vt[:, :].rearrange("p (c t) -> p c t", c=NC), nv[:, :, :], ACT.Silu).then_inc(S["g_silu"], 1)
                advance(nxt, st, min(4 * UNIT, cum["keys"]), free)
                act.wait_ge(S["unit_out"], units_before((GDN, h)) + 8)
                act.activation(sz[:, :], raw[:, 3, PAST:], ACT.Silu).then_inc(S["g_silu"], 1)
                for l in range(1, LEVELS):
                    advance(nxt, st, cum[f"b{l}"], free)
                for c in range(NC):
                    advance(nxt, st, cum[f"r{c}"], free)
                    if c:
                        act.wait_ge(S["g_qs"], 7 * h + c)
                        if c > 2:
                            act.wait_ge(S["g_o"], 8 * h + c - 1)
                        act.activation(carried[:, c % 2, 0:P], ps[:, 3, 0:P], ACT.Copy, scale=ht[:, T_E, c:c + 1])\
                            .then_inc(S["g_cq"], 1)
                        squares(S["g_o"], 8 * h, gu, xx[0], c - 1, S["g_osq"])
                squares(S["g_o"], 8 * h, gu, xx[0], NC - 1, S["g_osq"])
                advance(nxt, st, cum["end"], free)
                act.wait_ge(S["head_done"], h + 2)
                act.dma_start(mixed[bass.ds(h * P, P), :], mix[:, :]).then_inc(S["mix_stored"], 16)

            def mlstm(h, nxt):
                cum, st = plan(MLSTM, nxt and nxt[0]), [0]

                def free(b):
                    if b < 2:
                        act.wait_ge(S["m_qk"], 2 * h + b + 1)
                    elif b == 2:
                        act.wait_ge(S["m_v"], 2 * h + 2)
                    elif b == 4:
                        act.wait_ge(S["m_gate"], h + 1)

                act.wait_ge(S["head_done"], h + GH + 1)
                act.wait_ge(S["unit_out"], units_before((MLSTM, h)) + 10)
                for r in range(2):
                    act.activation(qk[:, :, 1 - r, :], raw[:, r, PAST:].rearrange("p (c t) -> p c t", c=NC), ACT.Copy)\
                        .then_inc(S["m_qk"], 1)
                act.activation(vt[:, :], raw[:, 3, PAST:], ACT.Sigmoid).then_inc(S["m_sig"], 1)
                act.activation(sz[:, :], raw[:, 4, PAST:], ACT.Sigmoid).then_inc(S["m_sig"], 1)
                advance(nxt, st, cum["decay"], free)
                for half in range(2):
                    act.wait_ge(S["m_decay"], 2 * h + half + 1)
                    act.activation(flat(dd)[:, SEQ + half * HALF:SEQ + (half + 1) * HALF], ps[:, 6 + half, :], ACT.Exp)\
                        .then_inc(S["m_exp"], 1)
                advance(nxt, st, cum["o"], free)
                for half in range(2):
                    act.wait_ge(S["m_o"], 2 * h + half + 1)
                    act.activation(flat(pair)[:, SEQ + half * HALF:SEQ + (half + 1) * HALF], ps[:, 2 + half, :], ACT.Copy)\
                        .then_inc(S["m_sg"], 1)
                for c in range(NC):
                    advance(nxt, st, cum[f"c{c}"], free)
                    if c:
                        act.wait_ge(S["m_qc"], 7 * h + c)
                        if c > 2:
                            act.wait_ge(S["m_nd"], 8 * h + c - 1)
                        act.activation(carried[:, c % 2, :], ps[:, 3, 0:P + 1], ACT.Copy, scale=ht[:, T_E, c:c + 1])\
                            .then_inc(S["m_cq"], 1)
                    if c == 5:
                        for i in range(4):
                            squares(S["m_h"], 8 * h, nv, dd_spare, i, S["m_hsq"])
                for i in range(4, NC):
                    squares(S["m_h"], 8 * h, nv, dd_spare, i, S["m_hsq"])
                advance(nxt, st, cum["end"], free)
                act.wait_ge(S["head_done"], h + GH + 2)
                act.dma_start(mixed[bass.ds(h * P + GW, P), :], mix[:, :]).then_inc(S["mix_stored"], 16)

            def weights_hi(k):
                half, i = divmod(k, KT)
                if k == 0:
                    act.wait_ge(S["o_load"], 32)
                if k == 3:
                    act.wait_ge(S["unit_done"], ALL_UNITS)
                if half == 1 and i % 2 == 0:
                    act.wait_ge(S[f"o_load{i // 2}"], 16)
                act.activation(wo_hi[half][i][:, :], wo_raw[half][:, i, :], ACT.Copy).then_inc(S["o_hi"], 1)

            def mixed_hi(pair, i):
                act.wait_ge(S[f"o_mx{i % 2}"], 16 * (2 * pair + i // 2 + 1))
                act.activation(mx_hi[i][:, :, :], mx_raw[i % 2][:, :, :], ACT.Copy).then_inc(S["o_mhi"], 1)

            def memory(h, nxt, more):
                cum, st = plan(MEM, nxt and nxt[0]), [0]

                def free(b):
                    if b == 0:
                        act.wait_ge(S["x_q"], h + 1)

                act.wait_ge(S["head_done"], h + GH + MH + 1)
                act.wait_ge(S["unit_out"], units_before((MEM, h)) + 4)
                act.activation(sz[:, :], raw[:, 1, PAST:], ACT.Silu).then_inc(S["x_silu"], 1)
                if nxt is not None:
                    advance(nxt, st, cum["scores"], free, more)
                else:
                    for k in range(3, 5):
                        weights_hi(k)
                for c in range(NC):
                    act.wait_ge(S["x_sc"], 4 * h + c // 2 + 1)
                    act.wait_ge(S["x_nb"], 4 * h + c // 2 + 1)
                    act.activation(flat(dd)[:, c * N_MEM:(c + 1) * N_MEM], ps[:, 2 + c // 2, (c % 2) * N_MEM:(c % 2 + 1) * N_MEM],
                                   ACT.Exp, scale=SCALE, bias=sm[:, 1, c:c + 1], accum_out=sm[:, 2, c:c + 1])\
                        .then_inc(S["x_p"], 1)
                if nxt is not None:
                    advance(nxt, st, cum["probs"], free, more)
                else:
                    for k in range(5, 7):
                        weights_hi(k)
                for q in range(4):
                    act.wait_ge(S["x_pt"], 4 * h + q + 1)
                    act.activation(flat(pair)[:, q * HALF:(q + 1) * HALF], ps[:, 4 + q, :], ACT.Copy)\
                        .then_inc(S["x_ptc"], 1)
                if nxt is not None and not more:
                    for k in range(3):
                        weights_hi(k)
                    mixed_hi(0, 0)
                if nxt is not None:
                    advance(nxt, st, cum["end"], free, more)
                else:
                    weights_hi(7)
                    mixed_hi(0, 1)
                act.wait_ge(S["head_done"], h + GH + MH + 2)
                act.dma_start(mixed[bass.ds(h * P + GW + MW, P), :], mix[:, :]).then_inc(S["mix_stored"], 16)

            with act.Fori(0, GH - 1) as h:
                gdn(h, (GDN, h + 1))
            gdn(GH - 1, (MLSTM, 0))
            with act.Fori(0, MH - 1) as h:
                mlstm(h, (MLSTM, h + 1))
            mlstm(MH - 1, (MEM, 0))
            with act.Fori(0, XH - 2) as h:
                memory(h, (MEM, h + 1), True)
            memory(XH - 2, (MEM, XH - 1), False)
            memory(XH - 1, None, False)

            for k in range(KT, 2 * KT):
                weights_hi(k)
            mixed_hi(0, 2)
            mixed_hi(0, 3)

            def out_pair(pair, ahead):
                def split(i):
                    if ahead:
                        act.wait_ge(S["o_used"], 4 * pair + i + 1)
                        mixed_hi(pair + 1, i)

                split(0)
                split(1)
                for r in range(2):
                    act.wait_ge(S["o_y"], 2 * pair + r + 1)
                    act.activation(y_sq[:, :], y[r][:, :], ACT.Square, accum_out=sm[:, 2, 0:1]).then_inc(S["o_sq"], 1)
                    split(2 + r)

            with act.Fori(0, NC // 2 - 1) as pair_n:
                out_pair(pair_n, True)
            out_pair(NC // 2 - 1, False)

        @block.vector
        def _(dve):
            def split_lo(slot, n):
                dve.wait_ge(w_hi_done[slot], n)
                dve.tensor_tensor(w_lo[slot][:, :, :], w_raw[slot][:, :, :], w_hi[slot][:, :, :].bitcast(F32),
                                  ALU.subtract).then_inc(w_split[slot], 1)

            def advance(nxt, st, upto, more=True):
                while (st[0] + 1) * UNIT <= upto:
                    u = st[0]
                    st[0] += 1
                    slot = SLOTS[nxt[0]][u // 2]
                    if u % 2 and slot < 2 and more:
                        split_lo(slot, uses(slot, nxt, u // 2) + 1)

            def scale(i):
                if i >= 2:
                    dve.wait_ge(S["x_turned"], 2 * (i - 1))
                dve.wait_ge(S["x_rstd"], i + 1)
                dve.wait_ge(S["grows1" if i < 2 else "grows0"], 16)
                dve.scalar_tensor_tensor(out=x_tok[:, i % 2, :], in0=x_in[:, i % 3, :],
                                         scalar=rstd_tiles[:, i:i + 1], in1=g_rows[:, 1 if i < 2 else 0, :],
                                         op0=ALU.mult, op1=ALU.mult).then_inc(S["x_scaled"], 1)

            scale(0)
            for i in range(2 + NC + 1):
                if i >= 1:
                    j = i - 1
                    hi, lo = ((mem_hi, mem_lo) if j < 2 else (xn_hi, xn_lo))
                    cols = slice(j * P, (j + 1) * P) if j < 2 else slice((j - 2) * P, (j - 1) * P)
                    for q in range(2):
                        dve.wait_ge(S["x_hi"], 2 * j + q + 1)
                        dve.tensor_tensor(lo[:, 4 * q:4 * q + 4, cols],
                                          ps[:, 4 + 2 * (j % 2) + q, :].rearrange("p (k t) -> p k t", k=4),
                                          hi[:, 4 * q:4 * q + 4, cols].bitcast(F32), ALU.subtract)\
                            .then_inc(S["x_lo"], 1)
                if i + 1 < 2 + NC:
                    scale(i + 1)
                if 1 <= i <= 2 * XH:
                    split_lo((i - 1) % 2, (i - 1) // 2 + 1)
                if i == 2 * XH + 1:
                    split_lo(2, 1)
            split_lo(0, KV_USES + 1)
            split_lo(1, KV_USES + 1)

            early = Steps(dve, S["early_dve"])
            dve.wait_ge(S["tiny"], 64)
            dve.wait_ge(S["gate_exp"], 1)
            dve.memset(gcol[0:32, 0:1], 1.0)
            dve.memset(gcol[32:64, 0:1], -1.0)
            dve.memset(gcol[32:64, 2:3], -1.0)
            dve.tensor_scalar(gcol[0:32, 2:3], gcol[0:32, 2:3], -1.0, None, ALU.mult)
            dve.tensor_scalar(gcol[32:64, 1:2], gcol[32:64, 1:2], -1.0, None, ALU.mult).then_inc(S["gate_m"], 1)
            dve.wait_ge(S["gate_act"], 1)
            dve.tensor_scalar(u_row[0:64, :], e_row[0:64, :], 1.0, None, ALU.add).then_inc(S["gate_rows"], 1)
            dve.wait_ge(S["gate_rows"], 1)
            early.done(dve.scalar_tensor_tensor(out=e_row[0:64, :], in0=u_row[0:64, :], scalar=1.0, in1=e_row[0:64, :],
                                                op0=ALU.subtract, op1=ALU.subtract))
            dve.wait_ge(S["gate_act"], 2)
            early.done(dve.tensor_tensor(l_row[0:64, :], l_row[0:64, :], e_row[0:64, :], ALU.subtract))
            early.done(dve.scalar_tensor_tensor(out=l_row[0:64, :], in0=z_row[0:64, :], scalar=0.0, in1=l_row[0:64, :],
                                                op0=ALU.max, op1=ALU.add))
            dve.tensor_scalar(i_row[32:64, :], i_row[32:64, :], gcol[32:64, 3:4], None, ALU.add)
            early.done(dve.tensor_scalar(rows[0:64, :], l_row[0:64, :], gcol[0:64, 2:3], None, ALU.mult))
            mh = slice(R_MF, R_MF + MH)
            early.done(dve.tensor_tensor_scan(m_row[mh, 1:SEQ + 1], rows[mh, :], i_row[mh, :], 0.0, ALU.add, ALU.max))
            early.done(dve.tensor_tensor(rows[mh, :], rows[mh, :], m_row[mh, 0:SEQ], ALU.add))
            dve.tensor_tensor(rows[mh, :], rows[mh, :], m_row[mh, 1:SEQ + 1], ALU.subtract)
            dve.tensor_tensor(rows[R_MI:R_MI + MH, :], i_row[mh, :], m_row[mh, 1:SEQ + 1], ALU.subtract)\
                .then_inc(S["gate_rows"], 1)
            st = [0]
            advance((GDN, 0), st, UNITS[GDN] * UNIT)
            dve.wait_ge(S["params_turned"], 1)
            dve.tensor_copy(params[:, 0:79], ps[:, 7, 0:79]).then_inc(S["params_out"], 1)
            dve.wait_ge(S["gate_turned"], 2)
            gates = ps[:, 4:6, :].rearrange("p a (c r) -> p (a c) r", c=4)
            dve.tensor_copy(tab[:, 0:GH, T_G, :].rearrange("p h c -> p c h"), gates[:, :, R_GA:R_GA + GH])
            dve.tensor_copy(tab[:, GH:, T_G, :].rearrange("p h c -> p c h"), gates[:, :, R_MF:R_MF + MH])
            eb = sm[:, 0:3, :].rearrange("p a b -> p (a b)")
            dve.tensor_scalar(eb.rearrange("p (h c) -> p c h", c=NC), gates[:, :, R_GB:R_GB + GH], 1.0, None, ALU.add)\
                .then_inc(S["gate_tab"], 1)
            dve.wait_ge(S["gate_tab"], 1)
            dve.reciprocal(tab[:, 0:GH, T_X, :], eb.rearrange("p (h c) -> p h c", c=NC))
            dve.wait_ge(S["gate_exp"], 2)
            dve.tensor_scalar(tab[:, GH:, T_X, :], tab[:, GH:, T_X, :], SCALE, None, ALU.mult)
            dve.wait_ge(S["gate_exp"], 3)
            dve.tensor_scalar(tab[:, :, T_NE, :], tab[:, :, T_E, :], -1.0, None, ALU.mult).then_inc(S["head_done"], 1)
            dve.wait_ge(S["head_done"], 1)

            LAG = 12

            def finish(H, ot, base, gain):
                dve.wait_ge(S["mix_stored"], 16 * (H + 1))
                for half in range(2):
                    cols = slice(half * HALF, (half + 1) * HALF)
                    dve.wait_ge(ot, base + half + 1)
                    if gain is None:
                        ins = dve.tensor_tensor(mix[:, cols], ps[:, 2 + half, :], sz[:, cols], ALU.mult)
                    else:
                        ins = dve.scalar_tensor_tensor(out=mix[:, cols], in0=ps[:, 2 + half, :], scalar=gain,
                                                       in1=sz[:, cols], op0=ALU.mult, op1=ALU.mult)
                ins.then_inc(S["head_done"], 1)

            def split_log_decay(H, step):
                g = tab[:, bass.ds(H, 1), T_G, :].rearrange("p a c -> p (a c)")
                step.done(dve.tensor_copy(g_hi[:, :], g))
                dve.tensor_tensor(g_lo[:, :], g, g_hi[:, :].bitcast(F32), ALU.subtract)

            GDN_STEPS = 14

            def gdn(h, nxt):
                cum, st = plan(GDN, nxt and nxt[0]), [0]
                step = Steps(dve, S["g_dve"], h * GDN_STEPS)

                def mean_square(half):
                    c4 = slice(4 * half, 4 * half + 4)
                    dve.wait_ge(S["g_osq"], 8 * h + 4 * half + 4)
                    step.done(dve.tensor_tensor(sm[:, 9, c4], sm[:, 9, c4], sm[:, 8, c4], ALU.mult))
                    dve.tensor_scalar(sm[:, 5, c4], sm[:, 9, c4], 1.0 / P, EPS, ALU.mult, ALU.add).then_inc(S["g_oms"], 1)

                def normalise(half):
                    c4 = slice(4 * half, 4 * half + 4)
                    dve.wait_ge(S["g_ors"], 2 * h + half + 1)
                    step.done(dve.tensor_tensor(sm[:, 10, c4], sm[:, 6, c4], sm[:, 7, c4], ALU.mult))
                    dve.tensor_tensor(fk[:, c4, :], gu[:, c4, :], over(sm[:, 10, c4], P), ALU.mult).then_inc(S["g_og"], 1)

                dve.wait_ge(S["head_done"], h + 1)
                dve.tensor_copy(hconv[:, :], params[:, 0:72].rearrange("p (g h) -> p g h", h=GH)[:, :, bass.ds(h, 1)]
                                .rearrange("p g a -> p (g a)"))
                split_log_decay(h, step)
                dve.tensor_copy(ht[:, :, :], tab[:, bass.ds(h, 1), :, :].rearrange("p a k c -> p (a k) c"))\
                    .then_inc(S["g_tab"], 1)
                dve.wait_ge(S["g_tab"], h + 1)
                for b, dst in enumerate((flat(pair)[:, 0:SEQ], flat(pair)[:, SEQ:],
                                         nv[:, :, :].rearrange("p c t -> p (c t)"))):
                    if b == 0:
                        dve.wait_ge(S["unit_out"], units_before((GDN, h)) + 2)
                        step.done(dve.tensor_scalar(dst, raw[:, b, 0:SEQ], hconv[:, b:b + 1], None, ALU.mult))
                    else:
                        dve.wait_ge(S["g_tap"], 2 * h + b)
                    for tap in range(1, 4):
                        ins = dve.scalar_tensor_tensor(out=dst, in0=raw[:, b, tap:tap + SEQ],
                                                       scalar=hconv[:, 3 * tap + b:3 * tap + b + 1], in1=dst,
                                                       op0=ALU.mult, op1=ALU.add)
                        if tap < 3:
                            step.done(ins)
                    ins.then_inc(S["g_conv"], 1)
                if nxt[0] == MLSTM:
                    split_lo(2, uses(2, nxt, 2))
                advance(nxt, st, cum["queries"])
                dve.wait_ge(S["g_sq"], 2 * NC * (h + 1))
                dve.tensor_scalar(sm[:, 0, :], sm[:, 0, :], EPS, None, ALU.add).then_inc(S["g_sse"], 1)
                for half in range(2):
                    c4 = slice(4 * half, 4 * half + 4)
                    dve.tensor_tensor(fk[:, c4, :], ps[:, 4 + half, :].rearrange("p (c t) -> p c t", c=4),
                                      over(ht[:, T_F, c4], P), ALU.mult).then_inc(S["g_fk"], 1)
                dve.wait_ge(S["g_rk"], h + 1)
                root = sm[:, 1, :].rearrange("p (c two) -> p c two", two=2)
                sums = sm[:, 0, :].rearrange("p (c two) -> p c two", two=2)
                dve.tensor_tensor(sm[:, 4, 0:NC], sums[:, :, 0], root[:, :, 0], ALU.mult)
                dve.tensor_scalar(sm[:, 7, 0:NC], root[:, :, 1], SCALE, None, ALU.mult)
                step.done(dve.tensor_tensor(sm[:, 3, 0:NC], root[:, :, 0], root[:, :, 0], ALU.mult))
                dve.tensor_tensor(sm[:, 2, 0:NC], sm[:, 3, 0:NC], ht[:, T_X, :], ALU.mult).then_inc(S["g_w"], 1)
                step.done(dve.tensor_tensor(sm[:, 9, 0:NC], sm[:, 7, 0:NC], sm[:, 7, 0:NC], ALU.mult))
                dve.wait_ge(S["g_w"], h + 1)
                dve.wait_ge(S["g_dm"], h + 1)
                dve.tensor_tensor(dd[:, :, 0, :], dd[:, :, 1, :], over(sm[:, 2, 0:NC], P), ALU.mult).then_inc(S["g_dd"], 1)
                dve.wait_ge(S["g_dd"], h + 1)
                for i in range(4):
                    dve.wait_ge(S["g_kq"], 4 * h + i + 1)
                    dve.tensor_tensor(pair[:, 2 * i:2 * i + 2, :, :].rearrange("p c two t -> p (c two t)"), ps[:, 2 + i, :],
                                      dd[:, 2 * i:2 * i + 2, :, :].rearrange("p c two t -> p (c two t)"), ALU.mult)\
                        .then_inc(S["g_pair"], 1)
                for half in range(2):
                    c4 = slice(4 * half, 4 * half + 4)
                    dve.wait_ge(S["g_vt"], 2 * h + half + 1)
                    dve.tensor_tensor(nv[:, c4, :], ps[:, 2 + half, :].rearrange("p (c t) -> p c t", c=4),
                                      over(sm[:, 4, c4], P), ALU.mult).then_inc(S["g_nv"], 1)
                for l in range(LEVELS):
                    if l:
                        advance(nxt, st, cum[f"b{l}"] - LAG)
                    b = 1 << l
                    dve.wait_ge(S["g_a"], 7 * h + l + 1)
                    if l == LEVELS - 1:
                        dve.wait_ge(S["g_xz"], h + 1)
                    x_low = halves(x_of(l), l)[0]
                    mask = level_mask[:, l, :].rearrange("p (n b) -> p n b", b=b).unsqueeze(1)\
                        .broadcast_to([P, NC, 64 // b, b])
                    dve.tensor_tensor(x_low, packed(4, l), mask, ALU.mult).then_inc(S["g_x"], 1)
                    m_low = halves(minv, l)[0]
                    if l == 0:
                        dve.wait_ge(S["g_x"], 7 * h + 1)
                        dve.wait_ge(S["g_m0"], h + 1)
                        dve.tensor_tensor(m_low, x_low, m_low, ALU.add).then_inc(S["g_m"], 1)
                        continue
                    if l > 1:
                        dve.wait_ge(S["g_c"], 6 * h + l - 1)
                        turned = ps[:, 6:8, :].rearrange("p a (c n two b) -> p (a c) n two b", c=4, two=2, b=b // 2)
                        dve.tensor_copy(halves(minv_t, l - 1)[1], turned[:, :, :, 1, :]).then_inc(S["g_mt"], 1)
                    if l < LEVELS - 1:
                        dve.wait_ge(S["g_b"], 5 * h + l)
                        dve.tensor_tensor(m_low, packed(5, l), m_low, ALU.add).then_inc(S["g_m"], 1)
                mt_high = halves(minv_t, LEVELS - 1)[1]
                dve.wait_ge(S["g_c"], 6 * h + 6)
                dve.tensor_tensor(mt_high, packed(6, LEVELS - 1), mt_high, ALU.add).then_inc(S["g_mt"], 1)
                for c in range(NC):
                    advance(nxt, st, cum[f"r{c}"] - LAG)
                    if c:
                        dve.wait_ge(S["g_ks"], 7 * h + c)
                        dve.scalar_tensor_tensor(out=rhs[:, c % 2, :], in0=ps[:, 2, 0:P], scalar=ht[:, T_NE, c:c + 1],
                                                 in1=nv[:, c, :], op0=ALU.mult, op1=ALU.add).then_inc(S["g_r"], 1)
                    dve.wait_ge(S["g_y"], 8 * h + c + 1)
                    dve.tensor_scalar(zed[:, c % 2, :], ps[:, 4, 0:P], sm[:, 2, c:c + 1], None, ALU.mult)\
                        .then_inc(S["g_z"], 1)
                    if c < NC - 1:
                        dve.wait_ge(S["g_up"], 7 * h + c + 1)
                        if c == 0:
                            ins = dve.tensor_copy(state[:, 0:P], ps[:, 5, 0:P])
                        else:
                            ins = dve.scalar_tensor_tensor(out=state[:, 0:P], in0=state[:, 0:P], scalar=ht[:, T_L, c:c + 1],
                                                           in1=ps[:, 5, 0:P], op0=ALU.mult, op1=ALU.add)
                        ins.then_inc(S["g_s"], 1)
                    dve.wait_ge(S["g_att"], 8 * h + c + 1)
                    if c == 0:
                        ins = dve.tensor_copy(gu[:, 0, :], ps[:, 6, 0:P])
                    else:
                        dve.wait_ge(S["g_cq"], 7 * h + c)
                        ins = dve.tensor_tensor(gu[:, c, :], carried[:, c % 2, 0:P], ps[:, 6 + c % 2, 0:P], ALU.add)
                    ins.then_inc(S["g_o"], 1)
                    if c == 5:
                        mean_square(0)
                    if c == 6:
                        normalise(0)
                mean_square(1)
                normalise(1)
                assert step.n == GDN_STEPS, step.n
                finish(h, S["g_ot"], 2 * h, params[:, 72:73])
                advance(nxt, st, cum["end"])

            MLSTM_STEPS = 13

            def mlstm(h, nxt):
                cum, st = plan(MLSTM, nxt and nxt[0]), [0]
                step = Steps(dve, S["m_dve"], h * MLSTM_STEPS)
                sg = flat(pair)[:, SEQ:].rearrange("p (c t) -> p c t", c=NC)

                def gate(half):
                    c4 = slice(4 * half, 4 * half + 4)
                    dve.wait_ge(S["m_nd"], 8 * h + 4 * half + 4)
                    den = num_den[:, c4, P]
                    step.done(dve.scalar_tensor_tensor(out=sm[:, 0, c4], in0=den, scalar=-1.0, in1=den,
                                                       op0=ALU.mult, op1=ALU.max))
                    dve.wait_ge(S["m_sg"], 2 * h + 2)
                    for c in range(4 * half, 4 * half + 4):
                        dve.tensor_tensor(nv[:, c, :], num_den[:, c, 0:P], sg[:, c, :], ALU.mult).then_inc(S["m_h"], 1)
                    step.done(dve.tensor_tensor(sm[:, 1, c4], sm[:, 0, c4], hguard[:, c4], ALU.max))
                    step.done(dve.reciprocal(sm[:, 7, c4], sm[:, 1, c4]))
                    step.done(dve.tensor_tensor(sm[:, 9, c4], sm[:, 7, c4], sm[:, 7, c4], ALU.mult))

                def mean_square(half):
                    c4 = slice(4 * half, 4 * half + 4)
                    dve.wait_ge(S["m_hsq"], 8 * h + 4 * half + 4)
                    step.done(dve.tensor_tensor(sm[:, 9, c4], sm[:, 9, c4], sm[:, 8, c4], ALU.mult))
                    dve.tensor_scalar(sm[:, 5, c4], sm[:, 9, c4], 1.0 / P, EPS, ALU.mult, ALU.add).then_inc(S["m_ms"], 1)

                def normalise(half):
                    c4 = slice(4 * half, 4 * half + 4)
                    dve.wait_ge(S["m_rs"], 2 * h + half + 1)
                    step.done(dve.tensor_tensor(sm[:, 10, c4], sm[:, 6, c4], sm[:, 7, c4], ALU.mult))
                    dve.tensor_tensor(fk[:, c4, :], nv[:, c4, :], over(sm[:, 10, c4], P), ALU.mult).then_inc(S["m_og"], 1)

                dve.wait_ge(S["head_done"], h + GH + 1)
                dve.tensor_copy(hguard[:, :], guard[:, bass.ds(h, 1), :].rearrange("p a c -> p (a c)"))
                dve.tensor_copy(hnorm[:, :], params[:, bass.ds(h + 73, 1)])
                split_log_decay(h + GH, step)
                dve.tensor_copy(ht[:, :, :], tab[:, bass.ds(h + GH, 1), :, :].rearrange("p a k c -> p (a k) c"))\
                    .then_inc(S["m_tab"], 1)
                dve.wait_ge(S["m_tab"], h + 1)
                for half in range(2):
                    c4 = slice(4 * half, 4 * half + 4)
                    dve.wait_ge(S["m_v"], 2 * h + half + 1)
                    dve.tensor_tensor(v_ext[:, c4, 0:P], ps[:, 2 + half, :].rearrange("p (c t) -> p c t", c=4),
                                      over(ht[:, T_X, c4], P), ALU.mult).then_inc(S["m_ve"], 1)
                dve.tensor_copy(v_ext[:, :, P], ht[:, T_X, :]).then_inc(S["m_ve"], 1)
                if nxt[0] == MLSTM:
                    split_lo(2, uses(2, nxt, 2))
                advance(nxt, st, cum["pairs"] - LAG)
                dve.wait_ge(S["m_dd"], h + 1)
                for half in range(2):
                    dve.wait_ge(S["m_pair"], 2 * h + half + 1)
                    dve.tensor_tensor(flat(pair)[:, half * HALF:(half + 1) * HALF], ps[:, 4 + half, :],
                                      flat(dd)[:, half * HALF:(half + 1) * HALF], ALU.mult).then_inc(S["m_pm"], 1)
                for half in range(2):
                    c4 = slice(4 * half, 4 * half + 4)
                    dve.wait_ge(S["m_k"], 2 * h + half + 1)
                    dve.tensor_tensor(fk[:, c4, :], ps[:, 6 + half, :].rearrange("p (c t) -> p c t", c=4),
                                      over(ht[:, T_F, c4], P), ALU.mult).then_inc(S["m_fk"], 1)
                for c in range(NC):
                    advance(nxt, st, cum[f"c{c}"] - LAG)
                    if c < NC - 1:
                        dve.wait_ge(S["m_up"], 7 * h + c + 1)
                        if c == 0:
                            ins = dve.tensor_copy(state[:, :], ps[:, 5, 0:P + 1])
                        else:
                            ins = dve.scalar_tensor_tensor(out=state[:, :], in0=state[:, :], scalar=ht[:, T_L, c:c + 1],
                                                           in1=ps[:, 5, 0:P + 1], op0=ALU.mult, op1=ALU.add)
                        ins.then_inc(S["m_s"], 1)
                    dve.wait_ge(S["m_pv"], 8 * h + c + 1)
                    if c == 0:
                        ins = dve.tensor_copy(num_den[:, 0, :], ps[:, 6, 0:P + 1])
                    else:
                        dve.wait_ge(S["m_cq"], 7 * h + c)
                        ins = dve.tensor_tensor(num_den[:, c, :], carried[:, c % 2, :], ps[:, 6 + c % 2, 0:P + 1], ALU.add)
                    ins.then_inc(S["m_nd"], 1)
                    if c == 4:
                        gate(0)
                    if c == 5:
                        mean_square(0)
                    if c == 6:
                        normalise(0)
                gate(1)
                mean_square(1)
                normalise(1)
                assert step.n == MLSTM_STEPS, step.n
                finish(h + GH, S["m_ot"], 2 * h, hnorm[:, 0:1])
                advance(nxt, st, cum["end"])

            MEM_STEPS = 5

            def weights_lo(k):
                half, i = divmod(k, KT)
                dve.wait_ge(S["o_hi"], k + 1)
                dve.tensor_tensor(wo_lo[half][:, i, :], wo_raw[half][:, i, :],
                                  wo_hi[half][i][:, :].bitcast(F32), ALU.subtract).then_inc(S["o_lo"], 1)

            def mixed_lo(pair, i):
                dve.wait_ge(S["o_mhi"], 4 * pair + i + 1)
                dve.tensor_tensor(mx_lo[i][:, :, :], mx_raw[i % 2][:, :, :], mx_hi[i][:, :, :].bitcast(F32),
                                  ALU.subtract).then_inc(S["o_mlo"], 1)

            def memory(h, nxt, more):
                cum, st = plan(MEM, nxt and nxt[0]), [0]
                step = Steps(dve, S["x_dve"], h * MEM_STEPS)
                dve.wait_ge(S["x_v"], h + 1)
                dve.tensor_copy(vm[:, :, :].rearrange("p a t -> p (a t)"), ps[:, 2, 0:2 * P]).then_inc(S["x_vm"], 1)
                if nxt is None:
                    weights_lo(3)
                    weights_lo(4)
                for i in range(4):
                    dve.wait_ge(S["x_sc"], 4 * h + i + 1)
                    step.done(dve.tensor_reduce(sm[:, 0, 2 * i:2 * i + 2],
                                                ps[:, 2 + i, :].rearrange("p (c m) -> p c m", c=2), AX.X, ALU.max))
                    dve.tensor_scalar(sm[:, 1, 2 * i:2 * i + 2], sm[:, 0, 2 * i:2 * i + 2], -SCALE, None, ALU.mult)\
                        .then_inc(S["x_nb"], 1)
                if nxt is not None:
                    advance(nxt, st, cum["probs"] - LAG, more)
                dve.wait_ge(S["x_p"], 8 * h + 8)
                step.done(dve.reciprocal(sm[:, 3, 0:NC], sm[:, 2, 0:NC]))
                probs = flat(dd).rearrange("p (c m) -> p c m", c=NC)
                dve.tensor_tensor(probs, probs, over(sm[:, 3, 0:NC], N_MEM), ALU.mult).then_inc(S["x_pn"], 1)
                assert step.n == MEM_STEPS, step.n
                if nxt is None:
                    for k in range(5, KT):
                        weights_lo(k)
                    mixed_lo(0, 1)
                finish(h + GH + MH, S["x_o"], 2 * h, None)
                if nxt is not None and not more:
                    for k in range(3):
                        weights_lo(k)
                    mixed_lo(0, 0)
                if nxt is not None:
                    advance(nxt, st, cum["end"], more)

            with dve.Fori(0, GH - 1) as h:
                gdn(h, (GDN, h + 1))
            gdn(GH - 1, (MLSTM, 0))
            with dve.Fori(0, MH - 1) as h:
                mlstm(h, (MLSTM, h + 1))
            mlstm(MH - 1, (MEM, 0))
            with dve.Fori(0, XH - 2) as h:
                memory(h, (MEM, h + 1), True)
            memory(XH - 2, (MEM, XH - 1), False)
            memory(XH - 1, None, False)

            for k in range(KT, 2 * KT):
                weights_lo(k)
            mixed_lo(0, 2)
            mixed_lo(0, 3)
            dve.wait_ge(S["o_fg"], 16)

            def out_pair(pair, first, ahead):
                def split(i):
                    if ahead:
                        mixed_lo(pair + 1, i)

                split(0)
                split(1)
                for r in range(2):
                    dve.wait_ge(S[f"o_x{r}"], 16 * (pair + 1))
                    dve.wait_ge(S["o_used"], 4 * pair + r + 3)
                    if first and r:
                        dve.wait_ge(S["mix_stored"], 16 * (HEADS + 1))
                    if not first:
                        dve.wait_ge(S[f"o_st{r}"], 16 * pair)
                    dve.tensor_tensor(y[r][:, :], ps[:, 4 * r:4 * r + 2, :].rearrange("p a n -> p (a n)"), x_t[r][:, :],
                                      ALU.add).then_inc(S["o_y"], 1)
                    dve.wait_ge(S["o_sq"], 2 * pair + r + 1)
                    dve.tensor_scalar(sm[:, 0, 0:1], sm[:, 2, 0:1], 1.0 / D_MODEL, EPS, ALU.mult, ALU.add)\
                        .then_inc(S["o_ms"], 1)
                    dve.wait_ge(S["o_rs"], 2 * pair + r + 1)
                    dve.scalar_tensor_tensor(out=y[r][:, :], in0=y[r][:, :], scalar=sm[:, 1, 0:1], in1=fg_row[:, :],
                                             op0=ALU.mult, op1=ALU.mult).then_inc(S["o_out"], 1)
                    split(2 + r)

            out_pair(0, True, True)
            with dve.Fori(1, NC // 2 - 1) as pair_n:
                out_pair(pair_n, False, True)
            out_pair(NC // 2 - 1, False, False)

        @block.tensor
        def _(pe):
            def products(slot, xh, xl, cols, k, term):
                w = (w_hi, w_hi, w_lo)[term][slot]
                v = (xh, xl, xh)[term]
                return w[:, k, :], v[:, k, cols]

            def project(nxt, st, upto):
                kind = nxt[0]
                while st[0] < upto:
                    u, i = divmod(st[0], UNIT)
                    st[0] += 1
                    slot, half = SLOTS[kind][u // 2], u % 2
                    if i == 0:
                        if half == 0:
                            pe.wait_ge(w_split[slot], uses(slot, nxt, u // 2))
                        pe.wait_ge(S["unit_out"], units_before(nxt) + u - 1)
                    k, term = divmod(i, TERMS)
                    w, v = products(slot, xn_hi, xn_lo, slice(half * HALF, (half + 1) * HALF), k, term)
                    mm = pe.matmul(ps[:, half, :], w, v, start=(i == 0), stop=(i == UNIT - 1))
                    if i == UNIT - 1:
                        mm.then_inc(S["unit_done"], 1)

            pe.wait_ge(S["consts"], 1)
            for i in range(2 + NC):
                if i >= 2:
                    pe.wait_ge(S["x_lo"], 2 * (i - 1))
                pe.wait_ge(S["x_scaled"], i + 1)
                for q in range(2):
                    for k in range(4):
                        mm = pe.transpose(ps[:, 4 + 2 * (i % 2) + q, k * P:(k + 1) * P],
                                          x_tok[:, i % 2, (4 * q + k) * P:(4 * q + k + 1) * P], ident[:, :])
                    mm.then_inc(S["x_turned"], 1)
                if i >= 2:
                    b = i - 2
                    pe.wait_ge(w_split[b % 2], b // 2 + 1)
                    if b == 0:
                        pe.wait_ge(S["x_lo"], 4)
                    if b >= 2:
                        pe.wait_ge(S["unit_out"], b - 1)
                    for j in range(UNIT):
                        w, v = products(b % 2, mem_hi, mem_lo, slice(0, N_MEM), *divmod(j, TERMS))
                        mm = pe.matmul(ps[:, b % 2, 0:N_MEM], w, v, start=(j == 0), stop=(j == UNIT - 1))
                    mm.then_inc(S["unit_done"], 1)
            pe.wait_ge(w_split[2], 1)
            pe.wait_ge(S["x_lo"], 2 * (2 + NC))
            for half in range(2):
                pe.wait_ge(S["unit_out"], 2 * XH - 1 + half)
                for j in range(UNIT):
                    w, v = products(2, xn_hi, xn_lo, slice(half * HALF, (half + 1) * HALF), *divmod(j, TERMS))
                    mm = pe.matmul(ps[:, half, :], w, v, start=(j == 0), stop=(j == UNIT - 1))
                mm.then_inc(S["unit_done"], 1)
            pe.wait_ge(S["rowz_loaded"], 96)
            pe.transpose(ps[:, 7, 0:79], param_rows[0:79, :], ident[0:79, 0:79]).then_inc(S["params_turned"], 1)
            project((GDN, 0), [0], UNITS[GDN] * UNIT)
            pe.wait_ge(S["gate_rows"], 2)
            for half in range(2):
                for c in range(4 * half, 4 * half + 4):
                    mm = pe.transpose(ps[:, 4 + half, (c % 4) * P:(c % 4 + 1) * P], rows[:, c * P:(c + 1) * P], ident[:, :])
                mm.then_inc(S["gate_turned"], 1)
            for c in range(NC):
                mm = pe.transpose(ps[:, 6, c * 32:(c + 1) * 32], m_row[32:64, 1 + c * P:1 + (c + 1) * P], ident[32:64, 32:64])
            mm.then_inc(S["gate_turned"], 1)
            pe.wait_ge(S["gate_tab"], 1)
            pe.wait_ge(S["params_out"], 1)
            for i, lhs in enumerate((upper, later, ones)):
                mm = pe.matmul(ps[:, 7, i * 96:(i + 1) * 96], lhs[:, :], tab[:, :, T_G, :], start=(i == 0), stop=(i == 2),
                               skip_group_check=True)
            mm.then_inc(S["gate_sum"], 1)

            def decay(gu_ready, out):
                pe.wait_ge(*gu_ready)
                for half in range(2):
                    for part, g in enumerate((gu_hi, gu_lo)):
                        mm = pe.matmul(ps[:, 6 + half, :], later_r[:, :],
                                       g[:, 4 * half:4 * half + 4, :].rearrange("p c t -> p (c t)"),
                                       start=(part == 0), stop=(part == 1))
                    mm.then_inc(out, 1)

            def turn(og, h, ot):
                for half in range(2):
                    pe.wait_ge(og, 2 * h + half + 1)
                    for c in range(4 * half, 4 * half + 4):
                        mm = pe.transpose(ps[:, 2 + half, (c % 4) * P:(c % 4 + 1) * P], fk[:, c, :], ident[:, :])
                    mm.then_inc(ot, 1)

            def gdn(h, nxt):
                cum, st = plan(GDN, nxt and nxt[0]), [0]
                project(nxt, st, cum["decay"])
                decay((S["g_gu"], h + 1), S["g_decay"])
                project(nxt, st, cum["queries"])
                for r, turned in ((1, "g_qt"), (0, "g_kt")):
                    pe.wait_ge(S["g_silu"], 4 * h + 2 - r)
                    for half in range(2):
                        for c in range(4 * half, 4 * half + 4):
                            mm = pe.transpose(ps[:, 4 - 2 * r + half, (c % 4) * P:(c % 4 + 1) * P], qk[:, c, r, :],
                                              ident[:, :])
                        mm.then_inc(S[turned], 1)
                    if r:
                        project(nxt, st, cum["keys"])
                project(nxt, st, cum["pairs"])
                pe.wait_ge(S["g_sse"], h + 1)
                for i in range(4):
                    if i >= 2:
                        pe.wait_ge(S["g_fk"], 2 * h + i - 1)
                    for c in (2 * i, 2 * i + 1):
                        mm = pe.matmul(ps[:, 2 + i, (c % 2) * 2 * P:(c % 2 + 1) * 2 * P], qk[:, c, 0, :],
                                       qk[:, c, :, :].rearrange("p two t -> p (two t)"), start=(c % 2 == 0), stop=(c % 2 == 1),
                                       skip_group_check=True)
                    mm.then_inc(S["g_kq"], 1)
                pe.wait_ge(S["g_silu"], 4 * h + 3)
                for half in range(2):
                    pe.wait_ge(S["g_pair"], 4 * h + half + 1)
                    for c in range(4 * half, 4 * half + 4):
                        mm = pe.transpose(ps[:, 2 + half, (c % 4) * P:(c % 4 + 1) * P], vt[:, c * P:(c + 1) * P], ident[:, :])
                    mm.then_inc(S["g_vt"], 1)
                project(nxt, st, cum["a0"])
                for l in range(LEVELS):
                    if l == 0:
                        pe.wait_ge(S["g_pair"], 4 * h + 4)
                    else:
                        pe.wait_ge(S["g_m"], 6 * h + l)
                    for c in range(NC):
                        low = (ident[:, :].rearrange("p (n two b) -> p n two b", two=2, b=1)[:, :, 0, :] if l == 0
                               else halves_of(minv, c, l)[0])
                        mm = pe.matmul(ps[:, 4, c * 64:(c + 1) * 64], pair[:, c, 0, :], low,
                                       start=(c == 0), stop=(c == NC - 1), skip_group_check=True)
                    mm.then_inc(S["g_a"], 1)
                    if l == 0:
                        project(nxt, st, cum["a1"])
                        continue
                    if l > 1:
                        for c in range(NC):
                            mm = pe.transpose(ps[:, 6 + c // 4, (c % 4) * P:(c % 4 + 1) * P], minv[:, c, :], ident[:, :])
                        mm.then_inc(S["g_c"], 1)
                    project(nxt, st, cum[f"b{l}"])
                    pe.wait_ge(S["g_x"], 7 * h + l + 1)
                    if l == 1:
                        pe.wait_ge(S["g_mt0"], h + 1)
                    else:
                        pe.wait_ge(S["g_mt"], 6 * h + l - 1)
                    if l < LEVELS - 1:
                        for c in range(NC):
                            mm = pe.matmul(ps[:, 5, c * 64:(c + 1) * 64], minv_t[:, c, :], halves_of(x_of(l), c, l)[0],
                                           start=(c == 0), stop=(c == NC - 1), skip_group_check=True)
                        mm.then_inc(S["g_b"], 1)
                        project(nxt, st, cum[f"t{l}"])
                    else:
                        for c in range(NC):
                            mm = pe.matmul(ps[:, 6, c * 64:(c + 1) * 64], x_of(l)[:, c, :], halves_of(minv_t, c, l)[1],
                                           start=(c == 0), stop=(c == NC - 1), skip_group_check=True)
                        mm.then_inc(S["g_c"], 1)
                for c in range(NC):
                    project(nxt, st, cum[f"r{c}"])
                    if c:
                        pe.wait_ge(S["g_s"], 7 * h + c)
                        pe.matmul(ps[:, 2, 0:P], qk[:, c, 0, :], state[:, 0:P], start=True, stop=True).then_inc(S["g_ks"], 1)
                        if c > 1:
                            pe.wait_ge(S["g_cq"], 7 * h + c - 1)
                        pe.matmul(ps[:, 3, 0:P], qk[:, c, 1, :], state[:, 0:P], start=True, stop=True).then_inc(S["g_qs"], 1)
                    project(nxt, st, cum[f"y{c}"])
                    if c == 0:
                        pe.wait_ge(S["g_mt"], 6 * h + 6)
                        pe.wait_ge(S["g_nv"], 2 * h + 2)
                    else:
                        pe.wait_ge(S["g_r"], 7 * h + c)
                    pe.matmul(ps[:, 4, 0:P], minv_t[:, c, :], nv[:, 0, :] if c == 0 else rhs[:, c % 2, :],
                              start=True, stop=True).then_inc(S["g_y"], 1)
                    project(nxt, st, cum[f"s{c}"])
                    pe.wait_ge(S["g_z"], 8 * h + c + 1)
                    if c < NC - 1:
                        pe.matmul(ps[:, 5, 0:P], fk[:, c, :], zed[:, c % 2, :], start=True, stop=True).then_inc(S["g_up"], 1)
                    if c >= 2:
                        pe.wait_ge(S["g_o"], 8 * h + c - 1)
                    pe.matmul(ps[:, 6 + c % 2, 0:P], pair[:, c, 1, :], zed[:, c % 2, :], start=True, stop=True)\
                        .then_inc(S["g_att"], 1)
                project(nxt, st, cum["turn"])
                turn(S["g_og"], h, S["g_ot"])
                project(nxt, st, cum["end"])

            def mlstm(h, nxt):
                cum, st = plan(MLSTM, nxt and nxt[0]), [0]
                project(nxt, st, cum["v"])
                pe.wait_ge(S["head_done"], h + GH + 1)
                pe.wait_ge(S["unit_out"], units_before((MLSTM, h)) + 6)
                for half in range(2):
                    for c in range(4 * half, 4 * half + 4):
                        mm = pe.transpose(ps[:, 2 + half, (c % 4) * P:(c % 4 + 1) * P],
                                          raw[:, 2, PAST + c * P:PAST + (c + 1) * P], ident[:, :])
                    mm.then_inc(S["m_v"], 1)
                project(nxt, st, cum["decay"])
                decay((S["m_gu"], h + 1), S["m_decay"])
                project(nxt, st, cum["pairs"])
                pe.wait_ge(S["m_qk"], 2 * h + 2)
                for half in range(2):
                    for c in range(4 * half, 4 * half + 4):
                        mm = pe.matmul(ps[:, 4 + half, (c % 4) * P:(c % 4 + 1) * P], qk[:, c, 0, :], qk[:, c, 1, :],
                                       start=(c % 4 == 0), stop=(c % 4 == 3), skip_group_check=True)
                    mm.then_inc(S["m_pair"], 1)
                project(nxt, st, cum["k"])
                for half in range(2):
                    pe.wait_ge(S["m_exp"], 2 * h + half + 1)
                    for c in range(4 * half, 4 * half + 4):
                        mm = pe.transpose(ps[:, 6 + half, (c % 4) * P:(c % 4 + 1) * P], qk[:, c, 0, :], ident[:, :])
                    mm.then_inc(S["m_k"], 1)
                project(nxt, st, cum["o"])
                pe.wait_ge(S["m_sig"], 2 * h + 1)
                for half in range(2):
                    pe.wait_ge(S["m_ve"], 3 * h + half + 1)
                    for c in range(4 * half, 4 * half + 4):
                        mm = pe.transpose(ps[:, 2 + half, (c % 4) * P:(c % 4 + 1) * P], vt[:, c * P:(c + 1) * P], ident[:, :])
                    mm.then_inc(S["m_o"], 1)
                for c in range(NC):
                    project(nxt, st, cum[f"c{c}"])
                    if c == 0:
                        pe.wait_ge(S["m_fk"], 2 * h + 2)
                        pe.wait_ge(S["m_sg"], 2 * h + 2)
                        pe.wait_ge(S["m_ve"], 3 * h + 3)
                        pe.wait_ge(S["m_pm"], 2 * h + 2)
                    if c:
                        pe.wait_ge(S["m_s"], 7 * h + c)
                        if c > 1:
                            pe.wait_ge(S["m_cq"], 7 * h + c - 1)
                        pe.matmul(ps[:, 3, 0:P + 1], qk[:, c, 1, :], state[:, :], start=True, stop=True)\
                            .then_inc(S["m_qc"], 1)
                    if c < NC - 1:
                        pe.matmul(ps[:, 5, 0:P + 1], fk[:, c, :], v_ext[:, c, :], start=True, stop=True)\
                            .then_inc(S["m_up"], 1)
                    if c >= 2:
                        pe.wait_ge(S["m_nd"], 8 * h + c - 1)
                    pe.matmul(ps[:, 6 + c % 2, 0:P + 1], flat(pair)[:, c * P:(c + 1) * P], v_ext[:, c, :],
                              start=True, stop=True).then_inc(S["m_pv"], 1)
                project(nxt, st, cum["turn"])
                turn(S["m_og"], h, S["m_ot"])
                project(nxt, st, cum["end"])

            def out_products(i, k_tiles):
                r, half = i % 2, i // 2
                for k in k_tiles:
                    for cols in range(2):
                        for term in range(TERMS):
                            w = (mx_hi, mx_hi, mx_lo)[term][i][:, k, :]
                            v = wo_lo[half][:, k, :] if term == 1 else wo_hi[half][k]
                            v = v[:, cols * HALF:(cols + 1) * HALF]
                            mm = pe.matmul(ps[:, 4 * r + cols, :], w, v, start=(half == 0 and k == 0 and term == 0),
                                           stop=(half == 1 and k == KT - 1 and term == TERMS - 1))
                    if k == KT - 1:
                        mm.then_inc(S["o_used"], 1)

            def first_tile(a, b):
                if a == 0:
                    pe.wait_ge(S["o_mlo"], 1)
                    pe.wait_ge(S["unit_out"], ALL_UNITS)
                for k in range(a, b):
                    pe.wait_ge(S["o_lo"], k + 1)
                    out_products(0, [k])

            def memory(h, nxt):
                cum, st = plan(MEM, nxt and nxt[0]), [0]
                if nxt is not None:
                    project(nxt, st, cum["v"])
                pe.wait_ge(S["x_kv"], h + 1)
                for m in range(2):
                    mm = pe.transpose(ps[:, 2, m * P:(m + 1) * P], hkv[:, 1, m * P:(m + 1) * P], ident[:, :])
                mm.then_inc(S["x_v"], 1)
                if nxt is not None:
                    project(nxt, st, cum["scores"])
                else:
                    first_tile(0, 3)
                pe.wait_ge(S["x_vm"], h + 1)
                pe.wait_ge(S["x_q"], h + 1)
                for c in range(NC):
                    mm = pe.matmul(ps[:, 2 + c // 2, (c % 2) * N_MEM:(c % 2 + 1) * N_MEM], vt[:, c * P:(c + 1) * P],
                                   hkv[:, 0, :], start=(c % 2 == 0), stop=(c % 2 == 1), skip_group_check=True)
                    if c % 2:
                        mm.then_inc(S["x_sc"], 1)
                if nxt is not None:
                    project(nxt, st, cum["probs"])
                else:
                    first_tile(3, 5)
                pe.wait_ge(S["x_pn"], h + 1)
                for q in range(4):
                    for i in range(4 * q, 4 * q + 4):
                        m, c = divmod(i, NC)
                        mm = pe.transpose(ps[:, 4 + q, (i % 4) * P:(i % 4 + 1) * P],
                                          flat(dd)[:, c * N_MEM + m * P:c * N_MEM + (m + 1) * P], ident[:, :])
                    mm.then_inc(S["x_pt"], 1)
                if nxt is not None:
                    project(nxt, st, cum["out"])
                else:
                    first_tile(5, 7)
                pe.wait_ge(S["x_ptc"], 4 * h + 4)
                for half in range(2):
                    for m in range(2):
                        mm = pe.matmul(ps[:, 2 + half, :], vm[:, m, :],
                                       flat(pair)[:, m * SEQ + half * HALF:m * SEQ + (half + 1) * HALF],
                                       start=(m == 0), stop=(m == 1))
                    mm.then_inc(S["x_o"], 1)
                if nxt is not None:
                    project(nxt, st, cum["end"])

            with pe.Fori(0, GH - 1) as h:
                gdn(h, (GDN, h + 1))
            gdn(GH - 1, (MLSTM, 0))
            with pe.Fori(0, MH - 1) as h:
                mlstm(h, (MLSTM, h + 1))
            mlstm(MH - 1, (MEM, 0))
            with pe.Fori(0, XH - 1) as h:
                memory(h, (MEM, h + 1))
            memory(XH - 1, None)

            first_tile(7, KT)
            pe.wait_ge(S["o_mlo"], 2)
            out_products(1, range(KT))
            pe.wait_ge(S["o_mlo"], 3)
            for k in range(KT):
                pe.wait_ge(S["o_lo"], KT + k + 1)
                out_products(2, [k])
            pe.wait_ge(S["o_mlo"], 4)
            out_products(3, range(KT))
            with pe.Fori(1, NC // 2) as pair_n:
                for i in range(4):
                    pe.wait_ge(S["o_mlo"], 4 * pair_n + i + 1)
                    if i < 2:
                        pe.wait_ge(S["o_y"], 2 * pair_n + i - 1)
                    out_products(i, range(KT))


_INS = ["x", "mem", "norm_g", "w_in", "conv_w", "gdn_a_log", "gdn_dt_bias", "gdn_norm_g", "mlstm_i_bias",
        "mlstm_f_bias", "mlstm_norm_g", "mem_norm_g", "w_mem_kv", "w_out", "final_norm_g"]


def kernel(**inputs):
    import concourse.bacc as bacc
    from concourse.bass_utils import run_bass_kernel_spmd as run

    nc = bacc.Bacc("TRN2", target_bir_lowering=False, num_devices=1)
    arrays, args = {}, []
    for name in _INS:
        a = np.ascontiguousarray(inputs[name])
        arrays[f"in_{name}"] = a
        ap = nc.dram_tensor(f"in_{name}", a.shape, F32, kind="ExternalInput").ap()
        args.append(ap if name == "final_norm_g" else ap[0])
    out = nc.dram_tensor("out_0", (1, SEQ, D_MODEL), F32, kind="ExternalOutput").ap()[0]
    mixed = nc.dram_tensor("mixed", (MIX, SEQ), F32, kind="Internal").ap()
    build(nc, *args, out, mixed)
    r = run(nc, [arrays], core_ids=[0])
    return r.results[0]["out_0"]
```
